# Optimizing a Trainium2 kernel written in Bass

```python
import jax, jax.numpy as jnp
from jax import lax
import numpy as np

D_MODEL = 1024
BATCH = 1
SEQ = 256
DEPTH = 2

CHUNK = 64
Q_BLOCK = 128
HEAD_DIM = 64
N_HEADS_FOX = 6
N_HEADS_SB = 5
N_HEADS_DSA = 5
W_FOX = N_HEADS_FOX * HEAD_DIM
W_SB = N_HEADS_SB * HEAD_DIM
W_DSA = N_HEADS_DSA * HEAD_DIM
KV_LATENT = 128
N_IDX_HEADS = 4
IDX_DIM = 64
TOPK_MAX = 256
ROPE_THETA = 500000.0
ROPE_DIM = HEAD_DIM // 4
D_FF = 2816
N_BRANCH = 3
EPS = 1e-6
D_IN = 3 * W_FOX + N_HEADS_FOX + 3 * W_SB + W_DSA + KV_LATENT + N_IDX_HEADS * IDX_DIM + IDX_DIM + N_IDX_HEADS + N_BRANCH * D_MODEL


def _in_sizes():
    return [W_FOX, W_FOX, W_FOX, N_HEADS_FOX,
            W_SB, W_SB, W_SB,
            W_DSA, KV_LATENT, N_IDX_HEADS * IDX_DIM, IDX_DIM, N_IDX_HEADS,
            N_BRANCH * D_MODEL]

def _split_points():
    pts, acc = [], 0
    for s in _in_sizes()[:-1]:
        acc += s
        pts.append(acc)
    return pts

def rmsnorm(x, g):
    xf = x.astype(jnp.float32)
    y = xf * lax.rsqrt(jnp.mean(xf * xf, axis=-1, keepdims=True) + EPS)
    return (y * g.astype(jnp.float32)).astype(x.dtype)

def swiglu(h, w_gu, w_down):
    g, u = jnp.split(h @ w_gu, 2, axis=-1)
    return (jax.nn.silu(g) * u) @ w_down

def rope_tables(seq):
    pos = jnp.arange(seq, dtype=jnp.float32)
    inv = ROPE_THETA ** (-jnp.arange(0, ROPE_DIM, 2, dtype=jnp.float32) / ROPE_DIM)
    ang = pos[:, None] * inv[None, :]
    return jnp.cos(ang), jnp.sin(ang)

def partial_rope(x, cos, sin):
    half = ROPE_DIM // 2
    x1 = x[..., :half].astype(jnp.float32)
    x2 = x[..., half:ROPE_DIM].astype(jnp.float32)
    c = cos[None, :, None, :]
    s = sin[None, :, None, :]
    r1 = (x1 * c - x2 * s).astype(x.dtype)
    r2 = (x2 * c + x1 * s).astype(x.dtype)
    return jnp.concatenate([r1, r2, x[..., ROPE_DIM:]], axis=-1)

def forgetting_attention(q, k, v, f_logit):
    B, S, H, Dh = q.shape
    scale = Dh ** -0.5
    c = jnp.cumsum(jax.nn.log_sigmoid(f_logit.astype(jnp.float32)), axis=1)
    c = c.transpose(0, 2, 1)
    outs = []
    for start in range(0, S, Q_BLOCK):
        end = start + Q_BLOCK
        s = jnp.einsum('bqhd,bkhd->bhqk', q[:, start:end], k[:, :end]).astype(jnp.float32) * scale
        bias = c[:, :, start:end, None] - c[:, :, None, :end]
        t_pos = jnp.arange(start, end)
        s_pos = jnp.arange(end)
        mask = s_pos[None, :] <= t_pos[:, None]
        p = jax.nn.softmax(jnp.where(mask, s + bias, -jnp.inf), axis=-1)
        outs.append(jnp.einsum('bhqk,bkhd->bqhd', p.astype(v.dtype), v[:, :end]))
    return jnp.concatenate(outs, axis=1)

def stick_breaking_attention(q, k, v):
    B, S, H, Dh = q.shape
    scale = Dh ** -0.5
    outs = []
    for start in range(0, S, Q_BLOCK):
        end = start + Q_BLOCK
        z = jnp.einsum('bqhd,bkhd->bhqk', q[:, start:end], k[:, :end]).astype(jnp.float32) * scale
        t_pos = jnp.arange(start, end)
        s_pos = jnp.arange(end)
        mask = s_pos[None, :] < t_pos[:, None]
        log_1m = jnp.where(mask, jax.nn.log_sigmoid(-z), 0.0)
        acc = lax.cumsum(log_1m, axis=3, reverse=True) - log_1m
        a = jnp.where(mask, jnp.exp(jax.nn.log_sigmoid(z) + acc), 0.0)
        outs.append(jnp.einsum('bhqk,bkhd->bqhd', a.astype(v.dtype), v[:, :end]))
    return jnp.concatenate(outs, axis=1)

def dsa_attention(q, k, v, iq, ik, iw):
    B, S, H, Dh = q.shape
    scale = Dh ** -0.5
    chunk_id = jnp.arange(S) // CHUNK
    topk = min(TOPK_MAX, S // 4)
    outs = []
    for start in range(0, S, Q_BLOCK):
        end = start + Q_BLOCK
        kk = min(topk, end)
        q_chunk = chunk_id[start:end]
        rel = jax.nn.relu(jnp.einsum('bqhd,bkd->bqhk', iq[:, start:end], ik[:, :end]).astype(jnp.float32))
        score = jnp.einsum('bqhk,bqh->bqk', rel, iw[:, start:end].astype(jnp.float32))
        admissible = chunk_id[None, :end] <= q_chunk[:, None]
        score = jnp.where(admissible[None], score, -jnp.inf)
        _, sel = lax.top_k(score, kk)
        valid = chunk_id[sel] <= q_chunk[None, :, None]
        k_sel = jax.vmap(lambda kb, ib: kb[ib])(k[:, :end], sel)
        v_sel = jax.vmap(lambda vb, ib: vb[ib])(v[:, :end], sel)
        s = jnp.einsum('bqhd,bqkd->bqhk', q[:, start:end], k_sel).astype(jnp.float32) * scale
        p = jax.nn.softmax(jnp.where(valid[:, :, None, :], s, -jnp.inf), axis=-1)
        outs.append(jnp.einsum('bqhk,bqkd->bqhd', p.astype(v.dtype), v_sel))
    return jnp.concatenate(outs, axis=1)

def hybrid_mixer(h, w_in, b_forget, g_kv, w_kv_up, g_idx_k, w_up_fox, w_up_sb, w_up_dsa, w_out, cos, sin):
    B, S, _ = h.shape
    (q_a, k_a, v_a, f_a, q_b, k_b, v_b, q_c, c_kv, q_i, k_i, w_i, gates) = jnp.split(h @ w_in, _split_points(), axis=-1)
    heads = lambda t, n: t.reshape(B, S, n, HEAD_DIM)
    y_a = forgetting_attention(heads(q_a, N_HEADS_FOX), heads(k_a, N_HEADS_FOX), heads(v_a, N_HEADS_FOX), f_a + b_forget)
    y_b = stick_breaking_attention(heads(q_b, N_HEADS_SB), heads(k_b, N_HEADS_SB), heads(v_b, N_HEADS_SB))
    k_c, v_c = jnp.split(rmsnorm(c_kv, g_kv) @ w_kv_up, 2, axis=-1)
    q_c = partial_rope(heads(q_c, N_HEADS_DSA), cos, sin)
    k_c = partial_rope(k_c[:, :, None, :], cos, sin)[:, :, 0]
    q_i = partial_rope(q_i.reshape(B, S, N_IDX_HEADS, IDX_DIM), cos, sin)
    k_i = partial_rope(rmsnorm(k_i, g_idx_k)[:, :, None, :], cos, sin)[:, :, 0]
    y_c = dsa_attention(q_c, k_c, v_c, q_i, k_i, w_i)
    g_a, g_b, g_c = jnp.split(jax.nn.sigmoid(gates), N_BRANCH, axis=-1)
    merged = (g_a * (y_a.reshape(B, S, W_FOX) @ w_up_fox)
              + g_b * (y_b.reshape(B, S, W_SB) @ w_up_sb)
              + g_c * (y_c.reshape(B, S, W_DSA) @ w_up_dsa))
    return merged @ w_out

def first_inputs(seed: int = 0) -> dict:
    key = jax.random.key(seed)
    ks = jax.random.split(key, 20)
    f32 = jnp.float32
    nrm = lambda k, shape, fan_in: jax.random.normal(k, shape, f32) * (fan_in ** -0.5)
    gain = lambda k, shape: 1.0 + 0.02 * jax.random.normal(k, shape, f32)
    return {
        "x": jax.random.normal(ks[0], (BATCH, SEQ, D_MODEL), f32),
        "g_ffn1": gain(ks[1], (DEPTH, D_MODEL)),
        "w_ffn1_gu": nrm(ks[2], (DEPTH, D_MODEL, 2 * D_FF), D_MODEL),
        "w_ffn1_down": nrm(ks[3], (DEPTH, D_FF, D_MODEL), D_FF),
        "g_mix": gain(ks[4], (DEPTH, D_MODEL)),
        "w_in": nrm(ks[5], (DEPTH, D_MODEL, D_IN), D_MODEL),
        "b_forget": 2.0 + 0.5 * jax.random.normal(ks[6], (DEPTH, N_HEADS_FOX), f32),
        "g_kv_latent": gain(ks[7], (DEPTH, KV_LATENT)),
        "w_kv_up": nrm(ks[8], (DEPTH, KV_LATENT, 2 * HEAD_DIM), KV_LATENT),
        "g_idx_k": gain(ks[9], (DEPTH, IDX_DIM)),
        "w_up_fox": nrm(ks[10], (DEPTH, W_FOX, D_MODEL), W_FOX),
        "w_up_sb": nrm(ks[11], (DEPTH, W_SB, D_MODEL), W_SB),
        "w_up_dsa": nrm(ks[12], (DEPTH, W_DSA, D_MODEL), W_DSA),
        "w_out": nrm(ks[13], (DEPTH, D_MODEL, D_MODEL), D_MODEL),
        "g_ffn2": gain(ks[14], (DEPTH, D_MODEL)),
        "w_ffn2_gu": nrm(ks[15], (DEPTH, D_MODEL, 2 * D_FF), D_MODEL),
        "w_ffn2_down": nrm(ks[16], (DEPTH, D_FF, D_MODEL), D_FF),
        "g_final": gain(ks[17], (D_MODEL,)),
    }

def first_block(x, g_ffn1, w_ffn1_gu, w_ffn1_down, g_mix, w_in, b_forget, g_kv_latent, w_kv_up, g_idx_k,
              w_up_fox, w_up_sb, w_up_dsa, w_out, g_ffn2, w_ffn2_gu, w_ffn2_down, g_final):
    cos, sin = rope_tables(x.shape[1])
    for l in range(DEPTH):
        x = x + 0.5 * swiglu(rmsnorm(x, g_ffn1[l]), w_ffn1_gu[l], w_ffn1_down[l])
        x = x + hybrid_mixer(rmsnorm(x, g_mix[l]), w_in[l], b_forget[l], g_kv_latent[l], w_kv_up[l], g_idx_k[l],
                             w_up_fox[l], w_up_sb[l], w_up_dsa[l], w_out[l], cos, sin)
        x = x + 0.5 * swiglu(rmsnorm(x, g_ffn2[l]), w_ffn2_gu[l], w_ffn2_down[l])
    return rmsnorm(x, g_final)


SWA_Q_HEADS = 8
SWA_KV_HEADS = 2
SWA_WINDOW = 128
MOBA_HEADS = 8
MOBA_BLOCK = 256
MOBA_TOPK = 3
MOBA_Q_CHUNK = 32
D_FF_2 = 4 * D_MODEL
ROPE_THETA_2 = 10000.0
NORM_EPS = 1e-6
NEG_INF = -1e30

SWA_Q_W = SWA_Q_HEADS * HEAD_DIM
SWA_KV_W = SWA_KV_HEADS * HEAD_DIM
MOBA_W = MOBA_HEADS * HEAD_DIM
IN_SPLITS = [SWA_Q_W, SWA_KV_W, SWA_KV_W, MOBA_W, MOBA_W, MOBA_W, D_MODEL, D_MODEL]
IN_W = int(sum(IN_SPLITS))
IN_OFFSETS = [int(o) for o in np.cumsum(IN_SPLITS)[:-1]]


def rms_norm(x, gain):
    xf = x.astype(jnp.float32)
    y = xf * lax.rsqrt(jnp.mean(xf * xf, axis=-1, keepdims=True) + NORM_EPS)
    return (y * gain.astype(jnp.float32)).astype(x.dtype)

def rope(x, positions):
    half = HEAD_DIM // 2
    inv_freq = ROPE_THETA_2 ** (-jnp.arange(half, dtype=jnp.float32) / half)
    ang = positions.astype(jnp.float32)[..., None] * inv_freq
    cos = jnp.cos(ang)[:, :, None, :]
    sin = jnp.sin(ang)[:, :, None, :]
    xf = x.astype(jnp.float32)
    x1, x2 = xf[..., :half], xf[..., half:]
    out = jnp.concatenate([x1 * cos - x2 * sin, x2 * cos + x1 * sin], axis=-1)
    return out.astype(x.dtype)

def swa_attention(q, k, v, sinks):
    B, S = q.shape[:2]
    W = SWA_WINDOW
    nb = S // W
    G = SWA_Q_HEADS // SWA_KV_HEADS
    qb = q.reshape(B, nb, W, SWA_KV_HEADS, G, HEAD_DIM)

    def band(t):
        tb = t.reshape(B, nb, W, SWA_KV_HEADS, HEAD_DIM)
        prev = jnp.pad(tb[:, :-1], ((0, 0), (1, 0), (0, 0), (0, 0), (0, 0)))
        return jnp.concatenate([prev, tb], axis=2)

    kb, vb = band(k), band(v)
    s = jnp.einsum('bnqhgd,bnkhd->bnhgqk', qb, kb,
                   preferred_element_type=jnp.float32) * (HEAD_DIM ** -0.5)
    qi = jnp.arange(W)[:, None]
    kj = jnp.arange(2 * W)[None, :]
    diff = qi + W - kj
    blk = jnp.arange(nb)[:, None, None]
    valid = (diff >= 0) & (diff < W) & (blk * W - W + kj >= 0)
    s = jnp.where(valid[None, :, None, None], s, NEG_INF)
    sink = sinks.astype(jnp.float32).reshape(SWA_KV_HEADS, G)[None, None, :, :, None, None]
    sink = jnp.broadcast_to(sink, s.shape[:-1] + (1,))
    p = jax.nn.softmax(jnp.concatenate([s, sink], axis=-1), axis=-1)[..., :-1]
    o = jnp.einsum('bnhgqk,bnkhd->bnqhgd', p.astype(v.dtype), vb)
    return o.reshape(B, S, SWA_Q_W)

def _take_blocks(blocks, idx):
    return blocks[idx]

_gather_bh = jax.vmap(jax.vmap(_take_blocks))

def moba_attention(q, k, v):
    B, S = q.shape[:2]
    L = MOBA_BLOCK
    nblk = -(-S // L)
    s_pad = nblk * L
    pad = ((0, 0), (0, s_pad - S), (0, 0), (0, 0))
    kb = jnp.pad(k, pad).reshape(B, nblk, L, MOBA_HEADS, HEAD_DIM).transpose(0, 3, 1, 2, 4)
    vb = jnp.pad(v, pad).reshape(B, nblk, L, MOBA_HEADS, HEAD_DIM).transpose(0, 3, 1, 2, 4)
    k_mean = jnp.mean(kb.astype(jnp.float32), axis=3)
    qh = q.transpose(0, 2, 1, 3)
    gate = jnp.einsum('bhsd,bhnd->bhsn', qh.astype(jnp.float32), k_mean)
    qblk = jnp.arange(S) // L
    past = jnp.arange(nblk)[None, :] < qblk[:, None]
    gate = jnp.where(past[None, None], gate, NEG_INF)
    topk = min(MOBA_TOPK, nblk)
    _, sel = lax.top_k(gate, topk)
    sel_valid = sel < qblk[None, None, :, None]
    scale = HEAD_DIM ** -0.5
    QC = MOBA_Q_CHUNK
    n_chunks = S // QC

    def chunk(ci):
        start = ci * QC
        qc = lax.dynamic_slice_in_dim(qh, start, QC, axis=2)
        selc = lax.dynamic_slice_in_dim(sel, start, QC, axis=2)
        validc = lax.dynamic_slice_in_dim(sel_valid, start, QC, axis=2)
        kg = _gather_bh(kb, selc)
        vg = _gather_bh(vb, selc)
        s_sel = jnp.einsum('bhqd,bhqtld->bhqtl', qc, kg,
                           preferred_element_type=jnp.float32) * scale
        s_sel = jnp.where(validc[..., None], s_sel, NEG_INF).reshape(B, MOBA_HEADS, QC, topk * L)
        own = start // L
        k_own = lax.dynamic_index_in_dim(kb, own, axis=2, keepdims=False)
        v_own = lax.dynamic_index_in_dim(vb, own, axis=2, keepdims=False)
        s_own = jnp.einsum('bhqd,bhld->bhql', qc, k_own,
                           preferred_element_type=jnp.float32) * scale
        qpos = start + jnp.arange(QC)
        kpos = own * L + jnp.arange(L)
        s_own = jnp.where(kpos[None, :] <= qpos[:, None], s_own, NEG_INF)
        p = jax.nn.softmax(jnp.concatenate([s_sel, s_own], axis=-1), axis=-1).astype(v.dtype)
        p_sel = p[..., :topk * L].reshape(B, MOBA_HEADS, QC, topk, L)
        p_own = p[..., topk * L:]
        return (jnp.einsum('bhqtl,bhqtld->bhqd', p_sel, vg)
                + jnp.einsum('bhql,bhld->bhqd', p_own, v_own))

    out = lax.map(chunk, jnp.arange(n_chunks))
    return out.transpose(1, 0, 3, 2, 4).reshape(B, S, MOBA_W)

def adaln(h, shift, scale):
    return h * (1 + scale[:, None, :]) + shift[:, None, :]

def hybrid_layer(x, c, positions, g_mix, g_mlp, w_ada, b_ada, w_in, qn_swa, kn_swa,
                 qn_moba, kn_moba, sinks, w_o_swa, w_o_moba, w_out, w_up, w_down):
    B, S, _ = x.shape
    mod = jax.nn.silu(c) @ w_ada + b_ada
    sh1, sc1, gt1, sh2, sc2, gt2 = jnp.split(mod, 6, axis=-1)

    h = adaln(rms_norm(x, g_mix), sh1, sc1)
    proj = h @ w_in
    q_a, k_a, v_a, q_b, k_b, v_b, gate_a, gate_b = jnp.split(proj, IN_OFFSETS, axis=-1)
    q_a = rope(rms_norm(q_a.reshape(B, S, SWA_Q_HEADS, HEAD_DIM), qn_swa), positions)
    k_a = rope(rms_norm(k_a.reshape(B, S, SWA_KV_HEADS, HEAD_DIM), kn_swa), positions)
    v_a = v_a.reshape(B, S, SWA_KV_HEADS, HEAD_DIM)
    q_b = rope(rms_norm(q_b.reshape(B, S, MOBA_HEADS, HEAD_DIM), qn_moba), positions)
    k_b = rope(rms_norm(k_b.reshape(B, S, MOBA_HEADS, HEAD_DIM), kn_moba), positions)
    v_b = v_b.reshape(B, S, MOBA_HEADS, HEAD_DIM)
    y_a = swa_attention(q_a, k_a, v_a, sinks) @ w_o_swa
    y_b = moba_attention(q_b, k_b, v_b) @ w_o_moba
    mixed = jax.nn.sigmoid(gate_a) * y_a + jax.nn.sigmoid(gate_b) * y_b
    x = x + gt1[:, None, :] * (mixed @ w_out)

    h = adaln(rms_norm(x, g_mlp), sh2, sc2)
    u = jnp.square(jax.nn.relu(h @ w_up))
    x = x + gt2[:, None, :] * (u @ w_down)
    return x

def second_inputs(seed: int = 0) -> dict:
    key = jax.random.key(seed)
    ks = jax.random.split(key, 20)
    f32 = jnp.float32

    def nrm(k, shape, scale):
        return jax.random.normal(k, shape, f32) * scale

    x = jax.random.normal(ks[0], (BATCH, SEQ, D_MODEL), f32)
    c = jax.random.normal(ks[1], (BATCH, D_MODEL), f32)
    offs = jax.random.randint(ks[2], (BATCH, 1), 0, 1024, dtype=jnp.int32)
    positions = (jnp.arange(SEQ, dtype=jnp.int32)[None, :] + offs).astype(jnp.int32)
    return {
        "x": x,
        "c": c,
        "positions": positions,
        "rms_mix": 1.0 + nrm(ks[3], (DEPTH, D_MODEL), 0.05),
        "rms_mlp": 1.0 + nrm(ks[4], (DEPTH, D_MODEL), 0.05),
        "w_ada": nrm(ks[5], (DEPTH, D_MODEL, 6 * D_MODEL), 0.5 * D_MODEL ** -0.5),
        "b_ada": nrm(ks[6], (DEPTH, 6 * D_MODEL), 0.02),
        "w_in": nrm(ks[7], (DEPTH, D_MODEL, IN_W), D_MODEL ** -0.5),
        "q_norm_swa": 1.0 + nrm(ks[8], (DEPTH, HEAD_DIM), 0.05),
        "k_norm_swa": 1.0 + nrm(ks[9], (DEPTH, HEAD_DIM), 0.05),
        "q_norm_moba": 1.0 + nrm(ks[10], (DEPTH, HEAD_DIM), 0.05),
        "k_norm_moba": 1.0 + nrm(ks[11], (DEPTH, HEAD_DIM), 0.05),
        "swa_sinks": nrm(ks[12], (DEPTH, SWA_Q_HEADS), 0.5),
        "w_o_swa": nrm(ks[13], (DEPTH, SWA_Q_W, D_MODEL), SWA_Q_W ** -0.5),
        "w_o_moba": nrm(ks[14], (DEPTH, MOBA_W, D_MODEL), MOBA_W ** -0.5),
        "w_out": nrm(ks[15], (DEPTH, D_MODEL, D_MODEL), D_MODEL ** -0.5),
        "w_up": nrm(ks[16], (DEPTH, D_MODEL, D_FF_2), D_MODEL ** -0.5),
        "w_down": nrm(ks[17], (DEPTH, D_FF_2, D_MODEL), D_FF_2 ** -0.5),
    }

def second_block(x, c, positions, rms_mix, rms_mlp, w_ada, b_ada, w_in, q_norm_swa, k_norm_swa,
              q_norm_moba, k_norm_moba, swa_sinks, w_o_swa, w_o_moba, w_out, w_up, w_down):
    for l in range(DEPTH):
        x = hybrid_layer(x, c, positions, rms_mix[l], rms_mlp[l], w_ada[l], b_ada[l], w_in[l],
                         q_norm_swa[l], k_norm_swa[l], q_norm_moba[l], k_norm_moba[l],
                         swa_sinks[l], w_o_swa[l], w_o_moba[l], w_out[l], w_up[l], w_down[l])
    return x


def setup_inputs(seed=0):
    out = dict(first_inputs(seed))
    for name, value in second_inputs(seed + 1).items():
        if name != "x":
            out[name + "_2"] = value
    return out


def reference(
    x, g_ffn1, w_ffn1_gu, w_ffn1_down, g_mix, w_in, b_forget, g_kv_latent, w_kv_up, g_idx_k,
    w_up_fox, w_up_sb, w_up_dsa, w_out, g_ffn2, w_ffn2_gu, w_ffn2_down, g_final, c_2,
    positions_2, rms_mix_2, rms_mlp_2, w_ada_2, b_ada_2, w_in_2, q_norm_swa_2, k_norm_swa_2,
    q_norm_moba_2, k_norm_moba_2, swa_sinks_2, w_o_swa_2, w_o_moba_2, w_out_2, w_up_2, w_down_2,
):
    x = first_block(
        x, g_ffn1, w_ffn1_gu, w_ffn1_down, g_mix, w_in, b_forget, g_kv_latent, w_kv_up, g_idx_k,
        w_up_fox, w_up_sb, w_up_dsa, w_out, g_ffn2, w_ffn2_gu, w_ffn2_down, g_final,
    )
    return second_block(
        x, c_2, positions_2, rms_mix_2, rms_mlp_2, w_ada_2, b_ada_2, w_in_2, q_norm_swa_2,
        k_norm_swa_2, q_norm_moba_2, k_norm_moba_2, swa_sinks_2, w_o_swa_2, w_o_moba_2, w_out_2,
        w_up_2, w_down_2,
    )


_drawn_inputs = setup_inputs


def setup_inputs(seed=0):
    import zlib

    import numpy as np

    out = dict(_drawn_inputs(seed))
    spreads = {}
    factors = {'g_kv_latent': 7.096,
     'g_idx_k': 3.031,
     'g_ffn2': 4.048,
     'g_final': 2.805,
     'rms_mix_2': 8.0,
     'q_norm_swa_2': 8.0,
     'k_norm_swa_2': 8.0,
     'q_norm_moba_2': 8.0,
     'k_norm_moba_2': 8.0,
     'swa_sinks_2': 8.0}
    for name, (base, spread) in spreads.items():
        noise = np.random.default_rng([zlib.crc32(name.encode()), seed]).standard_normal(out[name].shape)
        drawn = base * np.exp(spread * noise) if base else spread * noise
        out[name] = __import__('jax').numpy.asarray(drawn.astype(out[name].dtype))
    for name, factor in factors.items():
        out[name] = (out[name] * factor).astype(out[name].dtype)
    return out
```

```python
from contextlib import ExitStack

import numpy as np

import concourse.bass as bass
from concourse import mybir

ALU = mybir.AluOpType
ACT = mybir.ActivationFunctionType
AX = mybir.AxisListType
F32 = mybir.dt.float32
F32R = mybir.dt.float32r
I32 = mybir.dt.int32

P = 128
SEQ, D, LAYERS = 256, 1024, 2
NT = SEQ // P
KD = D // P
HD = 64
EPS = 1e-6
SCALE = HD ** -0.5
MASKED = -1e30
PICKED = -3e38
TOPK = min(256, SEQ // 4)
CHUNK = 64
WINDOW = 128

FF1 = 2816 // P
FOX, SB, DSA, IDX = 6, 5, 5, 4
ROPE1 = 8
BRANCH1 = 3
YT1 = 9
FF2 = 4096 // P
SWA, MOBA = 8, 8
ROPE2 = 32
W_IN2 = 2304
YT2 = 8

TA, TB = 16, 8
PROJ1 = [(16, 8)] * 8
GATE1 = [(16, 8)] * 8
UP1 = [(16, 8)] * 3
OUT = [(16, 8), (16, 8), (16, 0)]
PROJ2 = [(16, 8)] * 6
GATE2 = [(16, 8)] * 5 + [(8, 0)]
UP2 = [(16, 8), (16, 8), (16, 0)]
SLOTS1 = [(16, 8)] * FF1 + PROJ1 + GATE1 + UP1 + OUT + [(16, 8)] * FF1
SLOTS2 = PROJ2 + GATE2 + UP2 + OUT + [(8, 8)] * FF2
assert len(SLOTS1) % 2 == 0 and len(SLOTS2) % 2 == 0

P1_G, P1_GKV, P1_BF, P1_GIDX, P1_WKV, P1_END = 0, 24, 25, 31, 95, 223
P2_G, P2_BADA, P2_QK, P2_SINK, P2_END = 0, 16, 64, 320, 328
C_ID, C_CAUSAL, C_STRICT, C_CHUNK, C_BAND, C_U, C_ROPE, C_INVF, C_END = (
    0, 128, 512, 896, 1280, 1664, 1920, 1952, 1984)
TWO_PI = (6.28125, 0.0019350051879882812, 3.0199159819567e-07)


def parts_before(slots, kind, n):
    return sum(1 for s in slots[:n] if s[kind])


class Walk:

    def __init__(self, slots, n0, count, group, groups_before):
        self.tiles = [(n, kind, i, i == slots[n][kind] - 1)
                      for n in range(n0, n0 + count) for kind in (0, 1) for i in range(slots[n][kind])]
        self.group = group
        self.mark = []
        g = groups_before
        for e in range(group - 1, len(self.tiles), group):
            n, kind, _, end = self.tiles[e]
            if end:
                self.mark.append(("ab"[kind], parts_before(slots, kind, n + 1)))
            else:
                g += 1
                self.mark.append(("g", g))
        self.groups_after = g


class Count:

    def __init__(self, eng, sem):
        self.eng, self.sem, self.n, self.loop = eng, sem, 0, None

    def value(self):
        return self.n if self.loop is None else self.loop + self.n

    def __call__(self, ins):
        ins.then_inc(self.sem, 1)
        self.n += 1
        self.eng.wait_ge(self.sem, self.value())

    def also(self, ins):
        ins.then_inc(self.sem, 1)
        self.n += 1


def feed_forward_steps(eng, tiles, step, chain=None):
    for j in range(3):
        step(j, j % 2)
    turns = (tiles - 5) // 2
    before = chain.n if chain else 0
    per = chain.per if chain else 0
    with eng.Fori(0, turns) as i:
        if chain:
            chain.loop = i * per
        for u in range(2):
            step(i * 2 + 3 + u, (3 + u) % 2)
    if chain:
        assert chain.n - before == per, (chain.n - before, per)
        chain.loop = None
        chain.n = before + per * turns
    for j in range(3 + 2 * turns, tiles):
        step(j, j % 2)


def schedule1():
    items = [("ckv", 0), ("fox", 0), ("kv", 0), ("fox", 1), ("turn", 0), ("turn", 1)]
    items += [("idx", h) for h in range(IDX)]
    items += [("turn", 2), ("turn", 3)]
    items += [("fox", h) for h in range(2, FOX)]
    items += [("sb", h) for h in range(SB)] + [("dsa", h) for h in range(DSA)]
    return items


def schedule2():
    items = [None, None, None, None, ("turn", 0), ("turn", 1), ("turn", 2)]
    items += [("swa", h) for h in range(2)] + [("turn", 3), ("turn", 4), ("turn", 5), ("turn", 6)]
    items += [("swa", h) for h in range(2, SWA)]
    items += [("moba", h) for h in range(MOBA)]
    return items


HEADS = ("fox", "sb", "dsa", "swa", "moba")
READ_BY = {"fox": "scores_taken", "sb": "scores_taken", "dsa": "scores_taken", "swa": "scores_taken",
           "moba": "scores_taken", "idx": "prep_copied", "ckv": "prep_copied", "kv": "prep_copied",
           "turn": "prep_copied"}


def heads_before(items, tick):
    back = [i for i in range(tick % 2, tick, 2) if items[i] and items[i][0] in HEADS]
    return count_upto(items, back[-1], lambda k: k in HEADS) if back else 0


def count_upto(items, tick, what):
    return sum(1 for x in items[:tick + 1] if x and what(x[0]))


def build(nc, a):
    with ExitStack() as ctx:
        start = 16512
        at = [start]

        def put(name, shape, dt=F32, where=None):
            size = int(np.prod(shape[1:])) * 4
            off = at[0] if where is None else where
            t = nc.alloc_sbuf_tensor_at(name, shape, dt, offset=off)
            if where is None:
                at[0] = off + (size + 31) // 32 * 32
            return t

        raw = [put(f"raw_{'ab'[k]}", [P, 2, (TA, TB)[k] * P]) for k in range(2)]
        whi = [put(f"weights_high_{'ab'[k]}", [P, 2, (TA, TB)[k] * P], F32R) for k in range(2)]
        wlo = [put(f"weights_low_{'ab'[k]}", [P, 2, (TA, TB)[k] * P], F32R) for k in range(2)]
        x = put("residual", [P, NT, D])
        hhi = put("h_high", [P, KD, SEQ], F32R)
        hlo = put("h_low", [P, KD, SEQ], F32R)
        consts = put("constants", [P, C_END])
        par = put("layer_parameters", [P, max(P1_END, P2_END)])
        small = put("small", [P, 64])
        ms = put("mean_squares", [P, 64])
        rs0 = put("rsqrt_guess", [P, 64])
        rt = put("rsqrt_temp", [P, 64])
        rstd = put("rstd", [P, 64])
        rowmax = put("negated_row_max", [P, 32, NT])
        rowsum = put("row_sums", [P, 32, NT])
        sinkexp = put("sink_exps", [P, 32, NT])
        csilu = put("silu_c", [P, KD])
        mod = put("modulation_columns", [P, 2, 48])
        ncol = put("norm_columns", [P, 2 * KD])
        rope2 = put("rope_tables_two", [P, NT, 2, ROPE2])
        mid = at[0]

        xn = put("x_normed", [P, NT, D], F32, mid)
        ex = put("exp_gate", [P, 2, SEQ], F32, mid + 8192)
        fd = put("one_plus_exp", [P, SEQ], F32, mid + 10240)
        fq = put("gate_part", [P, SEQ], F32, mid + 11264)
        fa = put("gated", [P, SEQ], F32, mid + 12288)
        ghi = put("gated_high", [P, 2, SEQ], F32R, mid + 13312)
        glo = put("gated_low", [P, 2, SEQ], F32R, mid + 15360)
        ada_w = put("ada_weights", [P, 2, KD, 512], F32, mid + 17408)
        ada_acc = put("ada_sums", [P, 2, 512], F32, mid + 17408 + 32768)
        at[0] = mid
        tok1 = put("tokens_one", [P, NT, 4, 384])
        qk1 = put("q_k_turned_one", [P, 4, 3, SEQ])
        g1 = put("gates_one", [P, 24, SEQ])
        y1 = put("y_one", [P, NT, YT1 * P])
        tt1 = put("turned_one", [P, 7, SEQ])
        dup1 = put("index_and_latent_keys", [P, NT, 2, P])
        kvt = put("latent_turned", [P, SEQ])
        kvv = put("latent_k_v", [P, NT, P])
        fsp = put("forget_softplus", [P, 3, NT, FOX])
        fcast = put("forget_cast", [P, FOX, NT, P])
        iscore = put("index_scores", [P, 384])
        selmask = put("selection_mask", [P, 384])
        top8 = put("top_eight", [P, 8])
        sm = put("scores", [P, 2, 384])
        aux = put("softplus", [P, 2, 384])
        run = put("stick_sums", [P, 384])
        pts = put("probs_turned", [P, 2, 384])
        rope_tmp = put("rope_temp", [P, 4, NT, 5, ROPE1])
        end1 = at[0]
        at[0] = mid
        tok2 = put("tokens_two", [P, NT, W_IN2])
        tt2 = put("turned_two", [P, 14, SEQ])
        g2 = put("gates_two", [P, 16, SEQ])
        y2 = put("y_two", [P, NT, YT2 * P])
        dup2 = put("window_keys_doubled", [P, NT, 2, P])
        sm2 = put("scores_two", [P, 2, 384])
        pts2 = put("probs_turned_two", [P, 2, 384])
        rope_tmp2 = put("rope_temp_two", [P, 4, 16 * ROPE2])
        sq2 = put("squares_two", [P, 1024])
        diag = put("gain_diagonals", [P, 4, P])
        end2 = at[0]
        gtb = put("residual_gain", [P, D], F32, max(end1, end2))
        gfin = put("final_gain", [P, D], F32, max(end1, end2) + 4096)
        assert max(end1, end2) + 8192 <= nc.sbuf_usable_end, (end1, end2)
        yhi = put("y_high", [P, YT1, SEQ], F32R, mid)
        ylo = put("y_low", [P, YT1, SEQ], F32R, mid + YT1 * SEQ * 4)
        mt = put("merge_terms", [P, 3, SEQ], F32, end2 - 3 * SEQ * 4 if end2 > end1 else end1 - 3 * SEQ * 4)

        ident = consts[:, C_ID:C_ID + P]
        ones = consts[:, C_U + P:C_U + 2 * P]

        def mask(c):
            return consts[:, c:c + 384]

        ps = ctx.enter_context(nc.psum_tensor("psum", [P, 8, 512], F32))

        def sem(name):
            return ctx.enter_context(nc.semaphore(name))

        land = [[sem(f"landed_{k}{u}") for u in range(2)] for k in "ab"]
        lo_ready = [sem("low_a_ready"), sem("low_b_ready")]
        layer_done, layer_open = sem("layer_done"), sem("layer_open")
        between, layers_closed = sem("between_blocks"), sem("layers_closed")
        params_in, ada_in = sem("params_in"), [sem("ada_in_0"), sem("ada_in_1")]
        setup_in, out_done = sem("setup_in"), sem("out_done")
        setup_chain, setup_vector = sem("setup_chain"), sem("setup_vector")
        first = sem("ada_sum")
        ada_sum = first
        hi_ready = [sem("high_a_ready"), sem("high_b_ready")]
        used = [sem("used_a"), sem("used_b")]
        group_done = sem("group_done")
        exp_ready, gated_ready = sem("exp_ready"), sem("gated_ready")
        x_ready, guess_ready, xn_ready = sem("x_ready"), sem("guess_ready"), sem("xn_ready")
        ms_ready = sem("ms_ready")
        turned, hhi_ready, hlo_ready = sem("turned"), sem("h_high_ready"), sem("h_low_ready")
        proj_copied = sem("proj_copied")
        scores_ready, scores_taken = sem("scores_ready"), sem("scores_taken")
        max_ready, probs_ready = sem("max_ready"), sem("probs_ready")
        abs_ready, log_ready, stick_ready = sem("abs_ready"), sem("log_ready"), sem("stick_ready")
        pt_ready, pt_copied, pv_ready, y_done = sem("pt_ready"), sem("pt_copied"), sem("pv_ready"), sem("y_done")
        prep_ready, prep_copied = sem("prep_ready"), sem("prep_copied")
        tokens_ready, index_added = sem("tokens_ready"), sem("index_added")
        tok_ask, tok_answer = sem("tokens_ask"), sem("tokens_answer")
        gate_exp, gates_ready = sem("gate_exp"), sem("gates_ready")
        merged_ready = sem("merged_ready")
        y_turned, yhi_ready, ylo_ready = sem("y_turned"), sem("y_high_ready"), sem("y_low_ready")
        ada_used = sem("ada_used")
        mod_ready = sem("mod_ready")
        diag_ready, spread, gain_copied = sem("diag_ready"), sem("spread"), sem("gain_copied")
        dve_chain, act_chain = sem("vector_chain"), sem("scalar_chain")
        last = act_chain
        cleared = range(first.num, last.num + 1)

        block = ctx.enter_context(nc.Block())

        segments = {
            1: [("ffn_a", FF1), ("proj", 8), ("gate", 8), ("up", 3), ("out", 3), ("ffn_b", FF1)],
            2: [("proj", 6), ("gate", 6), ("up", 3), ("out", 3), ("ffn", FF2)],
        }
        SL = {1: SLOTS1, 2: SLOTS2}

        def landed_before(blk, kind, parity):
            return LAYERS * sum(1 for n, s in enumerate(SLOTS1) if s[kind] and n % 2 == parity) if blk == 2 else 0

        def per_layer(blk, kind, parity):
            return sum(1 for n, s in enumerate(SL[blk]) if s[kind] and n % 2 == parity)

        def lo_before(blk, kind):
            return LAYERS * parts_before(SLOTS1, kind, len(SLOTS1)) if blk == 2 else 0

        @block.sync
        def _(sp):
            sp.dma_start(x[:, :, :], a["x"].rearrange("(t p) d -> p t d", p=P)).then_inc(setup_in, 16)
            sp.dma_start(consts[:, :], a["consts"]).then_inc(setup_in, 16)
            sp.dma_start(csilu[:, :], a["c"]).then_inc(setup_in, 16)
            sp.dma_start(small[:, 0:NT].bitcast(I32), a["positions"]).then_inc(setup_in, 16)
            sp.dma_start(gfin[:, :], a["g_final"]).then_inc(setup_in, 16)
            for blk in (1, 2):
                slots = SL[blk]
                with sp.Fori(0, LAYERS) as l:
                    n0 = 0
                    for name, count in segments[blk]:
                        def load(j, p, n0=n0, name=name):
                            static = isinstance(j, int)
                            for kind in (0, 1):
                                tiles = slots[n0 + j][kind] if static else slots[n0][kind]
                                if not tiles:
                                    continue
                                if not static:
                                    before = parts_before(slots, kind, n0) + j - 1
                                else:
                                    before = parts_before(slots, kind, n0 + j - 1) if n0 + j else -1
                                sp.wait_ge(lo_ready[kind], l * parts_before(slots, kind, len(slots))
                                           + before + (lo_before(blk, kind) + 2))
                                src = a[f"w{blk}_{name}_{'ab'[kind]}"]
                                sp.dma_start(raw[kind][:, p, 0:tiles * P],
                                             src[l, j, :, 0:tiles * P]).then_inc(land[kind][p], 16)

                        if name.startswith("ffn"):
                            load(0, n0 % 2)
                            load(1, (n0 + 1) % 2)
                            with sp.Fori(0, count // 2 - 1) as i:
                                for u in range(2):
                                    load(i * 2 + 2 + u, (n0 + u) % 2)
                        else:
                            for j in range(count):
                                load(j, (n0 + j) % 2)
                        n0 += count
            sp.wait_ge(layer_done, 3 * LAYERS * 2)
            sp.dma_start(a["out"].rearrange("(t p) d -> p t d", p=P), x[:, :, :]).then_inc(out_done, 16)
            sp.wait_ge(out_done, 16)

        @block.gpsimd
        def _(pool):
            pool.sem_inc(lo_ready[0], 2)
            pool.sem_inc(lo_ready[1], 2)
            for blk in (1, 2):
                with pool.Fori(0, LAYERS) as l:
                    width = P1_END if blk == 1 else P2_END
                    pool.dma_start(par[:, 0:width], a[f"params{blk}"][l]).then_inc(params_in, 16)
                    if blk == 2:
                        for c in range(12):
                            if c >= 2:
                                pool.wait_ge(ada_sum, c - 1)
                            pool.dma_start(ada_w[:, c % 2, :, :], a["w2_ada"][l, c]).then_inc(ada_in[c % 2], 16)
                    pool.wait_ge(layer_done, l * 3 + (3 + 3 * LAYERS * (blk - 1)))
                    pool.sem_inc(layers_closed, 1)
                    pool.sem_clear(cleared)
                    pool.sem_inc(layer_open, 1)

        def params_of(l, blk):
            return l * 16 + (16 if blk == 1 else 16 + 16 * LAYERS)

        def close_layer(eng, l, blk):
            eng.drain().then_inc(layer_done, 1)
            eng.wait_ge(layer_open, l + (1 + LAYERS * (blk - 1)))

        def turn_list(blk, order):
            return [[(i, source(blk, i), 64 if (blk, i) == (1, 6) else P) for i in pair] for pair in order]

        def source(blk, i):
            if blk == 1:
                if i < 2:
                    return lambda t: tok1[:, t, 3, P + i * P:P + (i + 1) * P]
                if i < 4:
                    return lambda t: dup1[:, t, i - 2, :]
                c = (i - 4) * P
                return lambda t: tok1[:, t, 2, c:min(c + P, DSA * HD)]
            if 4 <= i < 6:
                return lambda t: dup2[:, t, i - 4, :]
            c = i * P if i < 4 else 768 + (i - 6) * P
            return lambda t: tok2[:, t, c:c + P]

        TURNS = {1: turn_list(1, [(0, 1), (2, 3), (4, 5), (6,)]),
                 2: turn_list(2, [(0, 1), (4, 5), (2, 3), (6, 7), (10, 11), (8, 9), (12, 13)])}
        TURNED = {1: lambda i: (tt1[:, i, :], SCALE if i >= 4 else 1.0),
                  2: lambda i: (tt2[:, i, :], SCALE if i < 4 or 6 <= i < 10 else 1.0)}
        TOKENS = {1: {("ckv", 0): 1, ("turn", 0): 3, ("turn", 1): 5, ("turn", 2): 5, ("turn", 3): 5,
                      **{("fox", h): 2 for h in range(FOX)}},
                  2: {("turn", h): 1 if h < 3 else 2 for h in range(7)}}
        PREP = ("ckv", "kv", "turn", "idx")
        G_AT = {1: Walk(SLOTS1, FF1 + 8, 8, KD, Walk(SLOTS1, FF1, 4, KD, 0).groups_after + 8).groups_after,
                2: Walk(SLOTS2, 6, 6, KD, 12).groups_after}
        @block.tensor
        def _(pe):
            state = {}

            def mm3(out, l_hi, l_lo, r_hi, r_lo, start, stop):
                pe.matmul(out, l_hi, r_hi, start=start, stop=False, skip_group_check=True)
                pe.matmul(out, l_hi, r_lo, start=False, stop=False, skip_group_check=True)
                return pe.matmul(out, l_lo, r_hi, start=False, stop=stop, skip_group_check=True)

            def wait_part(l, blk, kind, n):
                slots = SL[blk]
                count = n if not isinstance(n, int) else parts_before(slots, kind, n + 1) - 1
                pe.wait_ge(lo_ready[kind], l * parts_before(slots, kind, len(slots))
                           + lo_before(blk, kind) + count + 3)

            def wait_ffn_part(l, blk, kind, n0, j):
                slots = SL[blk]
                pe.wait_ge(lo_ready[kind], l * parts_before(slots, kind, len(slots))
                           + lo_before(blk, kind) + parts_before(slots, kind, n0) + j + 3)

            def norm():
                for b in range(4):
                    for k in (2 * b, 2 * b + 1):
                        for t in range(NT):
                            if b == 0 and k == 0:
                                state["xn"] = state.get("xn", 0) + 1
                                pe.wait_ge(xn_ready, state["xn"])
                            m = pe.transpose(ps[:, b, (k % 2) * SEQ + t * P:(k % 2) * SEQ + (t + 1) * P],
                                             xn[:, t, k * P:(k + 1) * P], ident)
                    m.then_inc(turned, 1)
                state["norms"] = state.get("norms", 0) + 1
                state["h_waited"] = 0

            def need_h(k):
                if state["h_waited"] < k // 2 + 1:
                    state["h_waited"] = k // 2 + 1
                    pe.wait_ge(hlo_ready, 4 * (state["norms"] - 1) + k // 2 + 1)

            def feed_forward(l, blk, n0, tiles, gates):
                state.setdefault("gated", 0)
                g0 = state["gated"]

                def gate_up(j, p):
                    wait_ffn_part(l, blk, 0, n0, j)
                    for m in range(gates):
                        for k in range(KD):
                            if isinstance(j, int) and j == 0:
                                need_h(k)
                            c = (m * KD + k) * P
                            last_mm = mm3(ps[:, p, m * SEQ:(m + 1) * SEQ], whi[0][:, p, c:c + P], wlo[0][:, p, c:c + P],
                                          hhi[:, k, :], hlo[:, k, :], k == 0, k == KD - 1)
                    last_mm.then_inc(used[0], 1)

                def down(j, p, first_tile, last_tile):
                    wait_ffn_part(l, blk, 1, n0, j)
                    pe.wait_ge(gated_ready, g0 + j + 1)
                    if first_tile and blk == 2:
                        pe.wait_ge(gain_copied, 4)
                    for t in range(NT):
                        for h in range(2):
                            last_mm = mm3(ps[:, 4 + 2 * t + h, :], ghi[:, p, t * P:(t + 1) * P],
                                          glo[:, p, t * P:(t + 1) * P],
                                          whi[1][:, p, h * 512:(h + 1) * 512], wlo[1][:, p, h * 512:(h + 1) * 512],
                                          first_tile, last_tile)
                    last_mm.then_inc(used[1], 1)

                def step(j, p):
                    gate_up(j, p)
                    if not (isinstance(j, int) and j == 0):
                        down(j - 1, 1 - p, isinstance(j, int) and j == 1, False)

                feed_forward_steps(pe, tiles, step)
                down(tiles - 1, (tiles - 1) % 2, False, True)
                state["gated"] += tiles

            def enter(l, blk, tile):
                n, kind, i, end = tile
                if i == 0:
                    wait_part(l, blk, kind, n)

            def finish(m, mark_is_group, tile):
                if tile[3]:
                    m.then_inc(used[tile[1]], 1)
                elif mark_is_group:
                    m.then_inc(group_done, 1)

            def weight(tile):
                n, kind, i, _ = tile
                return whi[kind][:, n % 2, i * P:(i + 1) * P], wlo[kind][:, n % 2, i * P:(i + 1) * P]

            def gate_tile(l, blk, walk, g):
                if g >= 2:
                    pe.wait_ge(gate_exp, g - 1)
                for k in range(KD):
                    tile = walk.tiles[g * KD + k]
                    enter(l, blk, tile)
                    hi, lo = weight(tile)
                    m = mm3(ps[:, g % 2, 0:SEQ], hi, lo, hhi[:, k, :], hlo[:, k, :], k == 0, k == KD - 1)
                    finish(m, k == KD - 1, tile)

            def project_turned(l, blk, walk, count):
                for g in range(count):
                    if g >= 4:
                        pe.wait_ge(proj_copied, g - 3)
                    for k in range(KD):
                        n, kind, _, _ = walk.tiles[g * KD + k]
                        need_h(k)
                        cols = (2, 1)[kind]
                        m_in = (g % 3) if kind == 0 else 0
                        if k == 0 and m_in == 0:
                            wait_part(l, blk, kind, n)
                        c = (k * cols + m_in) * P
                        m = mm3(ps[:, g % 4, 0:SEQ], whi[kind][:, n % 2, c:c + P], wlo[kind][:, n % 2, c:c + P],
                                hhi[:, k, :], hlo[:, k, :], k == 0, k == KD - 1)
                    if kind == 1 or m_in == 1:
                        m.then_inc(used[kind], 1)
                    else:
                        m.then_inc(group_done, 1)

            def project_rows(l, blk, n0, count, copied_before):
                g = copied_before
                for n in range(n0, n0 + count):
                    for kind in (0, 1):
                        wait_part(l, blk, kind, n)
                        w = (256, 128)[kind]
                        for t in range(NT):
                            if g >= 4:
                                pe.wait_ge(proj_copied, g - 3)
                            for k in range(KD):
                                need_h(k)
                                m = mm3(ps[:, g % 4, 0:w], hhi[:, k, t * P:(t + 1) * P], hlo[:, k, t * P:(t + 1) * P],
                                        whi[kind][:, n % 2, k * w:(k + 1) * w], wlo[kind][:, n % 2, k * w:(k + 1) * w],
                                        k == 0, k == KD - 1)
                            if t == NT - 1:
                                m.then_inc(used[kind], 1)
                            else:
                                m.then_inc(group_done, 1)
                            g += 1

            def bank_free(items, tick):
                back = tick - 2
                while back >= 0 and items[back] is None:
                    back -= 2
                if back >= 0:
                    kind = READ_BY[items[back][0]]
                    s = scores_taken if kind == "scores_taken" else prep_copied
                    pe.wait_ge(s, count_upto(items, back, lambda k: READ_BY[k] == kind))

            def scores(bank, qt, kt_, pb, forget):
                q, k_ = qt[pb:pb + HD, :], kt_[pb:pb + HD, :]
                pe.matmul(ps[:, bank, 0:P], q[:, 0:P], k_[:, 0:P], start=True, stop=forget is None, skip_group_check=True)
                if forget is not None:
                    pe.matmul(ps[:, bank, 0:P], fcast[:, forget, 0, :], consts[:, C_U:C_U + P],
                              start=False, stop=True, skip_group_check=True)
                m = pe.matmul(ps[:, bank, P:3 * P], q[:, P:SEQ], k_[:, 0:SEQ], start=True, stop=forget is None,
                              skip_group_check=True)
                if forget is not None:
                    pe.matmul(ps[:, bank, P:3 * P], fcast[:, forget, 0, :], consts[:, C_U:C_U + SEQ],
                              start=False, stop=False, skip_group_check=True)
                    m = pe.matmul(ps[:, bank, 2 * P:3 * P], fcast[:, forget, 1, :], consts[:, C_U:C_U + P],
                                  start=False, stop=True, skip_group_check=True)
                return m

            def item_scores(blk, items, tick):
                kind, h = items[tick]
                bank = 2 + tick % 2
                bank_free(items, tick)
                need = TOKENS[blk].get(items[tick])
                if need:
                    pe.wait_ge(tokens_ready, need)
                if kind in ("kv", "idx", "dsa", "swa", "moba"):
                    before = max(i for i in range(tick) if items[i] and items[i][0] in ("ckv", "kv", "turn"))
                    pe.wait_ge(prep_copied, count_upto(items, before, lambda k: k in PREP))
                m = None
                if kind == "fox":
                    m = scores(bank, qk1[:, 0, h // 2, :], qk1[:, 1, h // 2, :], HD * (h % 2), h)
                elif kind == "sb":
                    m = scores(bank, qk1[:, 2, h // 2, :], qk1[:, 3, h // 2, :], HD * (h % 2), None)
                elif kind == "idx":
                    m = scores(bank, tt1[:, h // 2, :], tt1[:, 2, :], HD * (h % 2), None)
                elif kind == "dsa":
                    m = scores(bank, tt1[:, 4 + h // 2, :], tt1[:, 3, :], HD * (h % 2), None)
                elif kind == "swa":
                    m = scores(bank, tt2[:, h // 2, :], tt2[:, 4 + h // 4, :], HD * (h % 2), None)
                elif kind == "moba":
                    m = scores(bank, tt2[:, 6 + h // 2, :], tt2[:, 10 + h // 2, :], HD * (h % 2), None)
                if kind in HEADS or kind == "idx":
                    if kind == "idx":
                        m.then_inc(prep_ready, 1)
                    else:
                        m.then_inc(scores_ready, 1)
                    return
                if kind == "ckv":
                    for t in range(NT):
                        m = pe.transpose(ps[:, bank, t * P:(t + 1) * P], tok1[:, t, 3, 0:P], ident)
                elif kind == "kv":
                    for t in range(NT):
                        m = pe.matmul(ps[:, bank, t * P:(t + 1) * P], kvt[:, t * P:(t + 1) * P],
                                      par[:, P1_WKV:P1_WKV + P], start=True, stop=True, skip_group_check=True)
                elif kind == "turn":
                    for i, src, w in TURNS[blk][h]:
                        for t in range(NT):
                            m = pe.transpose(ps[0:w, bank, (i % 2) * SEQ + t * P:(i % 2) * SEQ + (t + 1) * P],
                                             src(t), ident)
                m.then_inc(prep_ready, 1)

            def item_turn(blk, items, tick):
                if tick < 0 or tick >= len(items) or not items[tick] or items[tick][0] not in HEADS:
                    return
                e = count_upto(items, tick, lambda k: k in HEADS)
                pe.wait_ge(probs_ready, e)
                if e > 2:
                    pe.wait_ge(pt_copied, e - 2)
                s = (sm if blk == 1 else sm2)
                for b in range(3):
                    m = pe.transpose(ps[:, 4 + e % 2, b * P:(b + 1) * P], s[:, tick % 2, b * P:(b + 1) * P], ident)
                m.then_inc(pt_ready, 1)

            def item_values(blk, items, tick):
                if tick < 0 or tick >= len(items) or not items[tick] or items[tick][0] not in HEADS:
                    return
                kind, h = items[tick]
                e = count_upto(items, tick, lambda k: k in HEADS)
                pe.wait_ge(pt_copied, e)
                if e > 2:
                    pe.wait_ge(y_done, e - 2)
                q = (pts if blk == 1 else pts2)[:, e % 2, :]
                bank = 6 + e % 2

                def v(t):
                    if kind == "fox":
                        return tok1[:, t, 0, h * HD:(h + 1) * HD]
                    if kind == "sb":
                        return tok1[:, t, 1, h * HD:(h + 1) * HD]
                    if kind == "dsa":
                        return kvv[:, t, HD:2 * HD]
                    if kind == "swa":
                        return tok2[:, t, 640 + (h // 4) * HD:640 + (h // 4 + 1) * HD]
                    return tok2[:, t, 1792 + h * HD:1792 + (h + 1) * HD]

                pe.matmul(ps[:, bank, 0:HD], q[:, 0:P], v(0), start=True, stop=True, skip_group_check=True)
                pe.matmul(ps[:, bank, HD:2 * HD], q[:, P:2 * P], v(0), start=True, stop=False, skip_group_check=True)
                pe.matmul(ps[:, bank, HD:2 * HD], q[:, 2 * P:3 * P], v(1), start=False, stop=True,
                          skip_group_check=True).then_inc(pv_ready, 1)

            def ticks(l, blk, items, gates, walk):
                pe.wait_ge(proj_copied, 28 if blk == 1 else 24)
                if blk == 2:
                    pe.wait_ge(gain_copied, 2)
                for tick in range(max(len(items) + 2, gates)):
                    if tick < gates:
                        gate_tile(l, blk, walk, tick)
                    if tick < len(items) and items[tick]:
                        item_scores(blk, items, tick)
                    item_turn(blk, items, tick - 1)
                    item_values(blk, items, tick - 2)

            def turn_y(blk, tiles, heads):
                pe.wait_ge(y_done, heads)
                pe.wait_ge(gate_exp, 24 if blk == 1 else 16)
                y = y1 if blk == 1 else y2
                for i in range(tiles):
                    b = (i // 2) % 4
                    if i % 2 == 0 and i // 2 >= 4:
                        pe.wait_ge(ylo_ready, i // 2 - 3)
                    for t in range(NT):
                        m = pe.transpose(ps[:, b, (i % 2) * SEQ + t * P:(i % 2) * SEQ + (t + 1) * P],
                                         y[:, t, i * P:(i + 1) * P], ident)
                    if i % 2 == 1 or i == tiles - 1:
                        m.then_inc(y_turned, 1)

            def up_and_out(l, blk, up_walk, tiles, branches, out_n0):
                pe.wait_ge(ylo_ready, (tiles + 1) // 2)
                for f in range(KD):
                    if f >= 2:
                        pe.wait_ge(merged_ready, f - 1)
                    per = tiles // branches
                    for i in range(tiles):
                        tile = up_walk.tiles[f * tiles + i]
                        enter(l, blk, tile)
                        hi, lo = weight(tile)
                        br = i // per
                        bank = 4 + 2 * (f % 2) + br // 2
                        m = mm3(ps[:, bank, (br % 2) * SEQ:(br % 2 + 1) * SEQ], hi, lo, yhi[:, i, :], ylo[:, i, :],
                                i % per == 0, i % per == per - 1)
                        finish(m, i == tiles - 1, tile)
                pe.wait_ge(merged_ready, KD)
                kt_ = 0
                for n in range(out_n0, out_n0 + 3):
                    for kind in (0, 1):
                        rows = SL[blk][n][kind] // KD
                        if rows:
                            wait_part(l, blk, kind, n)
                        for r in range(rows):
                            for t in range(NT):
                                for h in range(2):
                                    c = r * D + h * 512
                                    m = mm3(ps[:, 4 + 2 * t + h, :], hhi[:, kt_, t * P:(t + 1) * P],
                                            hlo[:, kt_, t * P:(t + 1) * P], whi[kind][:, n % 2, c:c + 512],
                                            wlo[kind][:, n % 2, c:c + 512], kt_ == 0, kt_ == KD - 1)
                            kt_ += 1
                        if rows:
                            m.then_inc(used[kind], 1)

            def ada():
                for c in range(12):
                    pe.wait_ge(ada_sum, c + 1)
                    for i in range(4):
                        m = pe.matmul(ps[:, 7, 4 * c + i:4 * c + i + 1], ada_acc[:, c % 2, i * P:(i + 1) * P],
                                      ones[:, 0:1], start=True, stop=True, skip_group_check=True)
                    m.then_inc(ada_used, 1)

            def spread_gain(first_one):
                for h in range(2):
                    pe.wait_ge(diag_ready, h + 1 + (0 if first_one else 2))
                    pe.matmul(ps[:, 4 + h, :], ones, diag[:, :, :].rearrange("p a b -> p (a b)"),
                              start=True, stop=True, skip_group_check=True).then_inc(spread, 1)

            pe.wait_ge(setup_in, 80)
            for blk in (1, 2):
                with pe.Fori(0, LAYERS) as l:
                    state.clear()
                    if blk == 1:
                        norm()
                        feed_forward(l, 1, 0, FF1, 2)
                        norm()
                        w = Walk(SLOTS1, FF1, 4, KD, 0)
                        project_turned(l, 1, w, 12)
                        project_rows(l, 1, FF1 + 4, 4, 12)
                        pe.wait_ge(params_in, params_of(l, blk))
                        ticks(l, 1, schedule1(), 24, Walk(SLOTS1, FF1 + 8, 8, KD, 0))
                        turn_y(1, YT1, FOX + SB + DSA)
                        up_and_out(l, 1, Walk(SLOTS1, FF1 + 16, 3, YT1, 0), YT1, 3, FF1 + 19)
                        norm()
                        feed_forward(l, 1, FF1 + 22, FF1, 2)
                    else:
                        ada()
                        norm()
                        spread_gain(True)
                        project_rows(l, 2, 0, 6, 0)
                        ticks(l, 2, schedule2(), 16, Walk(SLOTS2, 6, 6, KD, 0))
                        turn_y(2, YT2, SWA + MOBA)
                        up_and_out(l, 2, Walk(SLOTS2, 12, 3, YT2, 0), YT2, 2, 15)
                        norm()
                        spread_gain(False)
                        feed_forward(l, 2, 18, FF2, 1)
                    close_layer(pe, l, blk)

        @block.scalar
        def _(act):
            chain = Count(act, act_chain)
            state = {}

            def seen(s, name, k=1):
                state[name] = state.get(name, 0) + k
                act.wait_ge(s, state[name])

            def split_high(l, blk, kind, n, p=None, j=None, n0=None):
                slots = SL[blk]
                if j is None:
                    if n >= len(slots) or not slots[n][kind]:
                        return
                    p, width = n % 2, slots[n][kind] * P
                    seq = sum(1 for i in range(n) if i % 2 == p and slots[i][kind])
                    reuse = parts_before(slots, kind, n - 1) if n >= 2 else 0
                else:
                    width = slots[n0][kind] * P
                    seq = sum(1 for i in range(n0) if i % 2 == 0 and slots[i][kind]) if p == 0 else \
                        sum(1 for i in range(n0) if i % 2 == 1 and slots[i][kind])
                    seq = seq + j[1]
                    reuse = parts_before(slots, kind, n0) + j[0] - 1
                act.wait_ge(land[kind][p], l * (16 * per_layer(blk, kind, p)) + seq * 16
                            + (16 * landed_before(blk, kind, p) + 16))
                if not isinstance(reuse, int) or reuse > 0:
                    act.wait_ge(used[kind], reuse)
                act.activation(whi[kind][:, p, 0:width], raw[kind][:, p, 0:width], ACT.Copy).then_inc(hi_ready[kind], 1)

            def norm(cols, shifts=None):
                for t in range(NT):
                    seen(x_ready, "x", 2)
                    chain(act.activation(xn[:, t, :], x[:, t, :], ACT.Square, accum_out=ms[:, t:t + 1]))
                rsqrt(NT, 1.0 / D)
                state["norms"] = state.get("norms", 0) + 1
                for b in range(4):
                    seen(turned, "turned")
                    for k in (2 * b, 2 * b + 1):
                        m = act.activation(hhi[:, k, :], ps[:, b, (k % 2) * SEQ:(k % 2 + 1) * SEQ], ACT.Identity,
                                           scale=cols(k), bias=0.0 if shifts is None else shifts(k))
                        if k % 2 == 0:
                            chain.also(m)
                    m.then_inc(hhi_ready, 1)

            def rsqrt(width, scale):
                chain(act.activation(rs0[:, 0:width], ms[:, 0:width], ACT.Ln, scale=scale, bias=eps))
                act.activation(rs0[:, 0:width], rs0[:, 0:width], ACT.Exp, scale=-0.5).then_inc(guess_ready, 1)

            eps = small[:, 60:61]

            def feed_forward(l, blk, n0, tiles, gates):
                def step(j, p):
                    act.wait_ge(used[0], j + (n0 + 1))
                    if gates == 2:
                        act.activation(ex[:, p, :], ps[:, p, 0:SEQ], ACT.Exp, scale=-1.0).then_inc(exp_ready, 1)
                    else:
                        act.activation(ex[:, p, :], ps[:, p, 0:SEQ], ACT.Relu).then_inc(exp_ready, 1)
                    if isinstance(j, int):
                        split_high(l, blk, 0, n0 + j + 2)
                        split_high(l, blk, 1, n0 + j + 1)
                    else:
                        i = state["i"]
                        u = 0 if p == 1 else 1
                        split_high(l, blk, 0, None, p, (j + 2, i + (2 if u == 0 else 3)), n0)
                        split_high(l, blk, 1, None, 1 - p, (j + 1, i + 2), n0)

                class Loop:
                    def Fori(self, lo, hi):
                        cm = act.Fori(lo, hi)

                        class Cm:
                            def __enter__(s):
                                state["i"] = cm.__enter__()
                                return state["i"]

                            def __exit__(s, *e):
                                return cm.__exit__(*e)
                        return Cm()

                feed_forward_steps(Loop(), tiles, step)

            def copy_projection(mark, out, src, scale):
                sem_, val = mark
                act.wait_ge({"a": used[0], "b": used[1], "g": group_done}[sem_], val)
                act.activation(out, src, ACT.Copy, scale=scale).then_inc(proj_copied, 1)

            def project_turned(l, blk, n0):
                w = Walk(SL[blk], n0, 4, KD, 0)
                for g in range(12):
                    s, m = g // 3, g % 3
                    if m == 0:
                        split_high(l, blk, 1, n0 + s + 1)
                    copy_projection(w.mark[g], qk1[:, s, m, :], ps[:, g % 4, 0:SEQ], SCALE if s in (0, 2) else 1.0)
                    if m == 1:
                        split_high(l, blk, 0, n0 + s + 2)
                return w.groups_after

            def project_rows(l, blk, n0, count, g, done_groups):
                for n in range(n0, n0 + count):
                    split_high(l, blk, 1, n + 1)
                    for kind in (0, 1):
                        for t in range(NT):
                            if t == NT - 1:
                                mark = ("ab"[kind], parts_before(SL[blk], kind, n + 1))
                            else:
                                done_groups += 1
                                mark = ("g", done_groups)
                            w = (256, 128)[kind]
                            if blk == 1:
                                out = tok1[:, t, n - n0, kind * 256:kind * 256 + w]
                            else:
                                c = (n - n0) * 384 + kind * 256
                                out = tok2[:, t, c:c + w]
                            copy_projection(mark, out, ps[:, g % 4, 0:w], 1.0)
                            g += 1
                        if kind == 0:
                            split_high(l, blk, 0, n + 2)
                return done_groups

            def item_softmax(blk, items, tick):
                kind, h = items[tick]
                s = (sm if blk == 1 else sm2)[:, tick % 2, :]
                bank = 2 + tick % 2
                if kind in ("fox", "dsa", "swa", "moba"):
                    e = count_upto(items, tick, lambda k: k in ("fox", "dsa", "swa", "moba"))
                    act.wait_ge(max_ready, e)
                    if kind == "swa":
                        chain.also(act.activation(sinkexp[:, tick, :], rowmax[:, tick, :], ACT.Exp,
                                                  bias=par[:, P2_SINK + h:P2_SINK + h + 1]))
                    chain.also(act.activation(s[:, 0:P], s[:, 0:P], ACT.Exp, bias=rowmax[:, tick, 0:1],
                                              accum_out=rowsum[:, tick, 0:1]))
                    act.activation(s[:, P:3 * P], s[:, P:3 * P], ACT.Exp, bias=rowmax[:, tick, 1:2],
                                   accum_out=rowsum[:, tick, 1:2]).then_inc(probs_ready, 1)
                elif kind == "sb":
                    e = count_upto(items, tick, lambda k: k == "sb")
                    act.wait_ge(stick_ready, e)
                    act.activation(s, s, ACT.Exp).then_inc(probs_ready, 1)

            def item_early(blk, items, tick):
                kind, h = items[tick]
                bank = 2 + tick % 2
                if kind == "sb":
                    e = count_upto(items, tick, lambda k: k == "sb")
                    act.wait_ge(abs_ready, e)
                    chain(act.activation(aux[:, tick % 2, :], aux[:, tick % 2, :], ACT.Exp, scale=-1.0))
                    act.activation(aux[:, tick % 2, :], aux[:, tick % 2, :], ACT.Ln, bias=1.0).then_inc(log_ready, 1)
                elif kind in ("ckv", "kv", "turn", "idx"):
                    e = count_upto(items, tick, lambda k: k in ("ckv", "kv", "turn", "idx"))
                    act.wait_ge(prep_ready, e)
                    if kind == "ckv":
                        act.activation(kvt[:, :], ps[:, bank, 0:SEQ], ACT.Identity,
                                       scale=par[:, P1_GKV:P1_GKV + 1]).then_inc(prep_copied, 1)
                    elif kind == "kv":
                        act.activation(kvv[:, :, :].rearrange("p t c -> p (t c)"), ps[:, bank, 0:SEQ],
                                       ACT.Copy).then_inc(prep_copied, 1)
                    elif kind == "idx":
                        if h >= 2:
                            act.wait_ge(index_added, h - 1)
                        act.activation(sm[:, tick % 2, :], ps[:, bank, 0:384], ACT.Relu).then_inc(prep_copied, 1)
                    else:
                        todo = TURNS[blk][h]
                        for q, (i, _, w) in enumerate(todo):
                            dst, scale = TURNED[blk](i)
                            m = act.activation(dst[0:w, :], ps[0:w, bank, (i % 2) * SEQ:(i % 2 + 1) * SEQ], ACT.Copy,
                                               scale=scale)
                            if q < len(todo) - 1:
                                chain.also(m)
                        m.then_inc(prep_copied, 1)

            def item_copy(blk, items, tick):
                if tick < 0 or tick >= len(items) or not items[tick] or items[tick][0] not in HEADS:
                    return
                e = count_upto(items, tick, lambda k: k in HEADS)
                act.wait_ge(pt_ready, e)
                act.activation((pts if blk == 1 else pts2)[:, e % 2, :], ps[:, 4 + e % 2, 0:384],
                               ACT.Copy).then_inc(pt_copied, 1)

            def gate_tile(blk, walk, tick, gates):
                mark = walk.mark[tick]
                act.wait_ge({"a": used[0], "b": used[1], "g": group_done}[mark[0]], mark[1])
                act.activation((g1 if blk == 1 else g2)[:, tick, :], ps[:, tick % 2, 0:SEQ], ACT.Exp,
                               scale=-1.0).then_inc(gate_exp, 1)

            def ticks(l, blk, items, gates, walk, n0):
                for tick in range(max(len(items) + 2, gates)):
                    item_copy(blk, items, tick - 1)
                    if tick < gates and tick % 3 == 0:
                        split_high(l, blk, 1, n0 + tick // 3 + 1)
                    if tick in TOKEN_WORK_ACT[blk]:
                        TOKEN_WORK_ACT[blk][tick]()
                    if tick < len(items) and items[tick]:
                        item_early(blk, items, tick)
                    if tick < gates:
                        gate_tile(blk, walk, tick, gates)
                        if tick % 3 == 1 or (blk == 2 and tick == 15):
                            split_high(l, blk, 0, n0 + tick // 3 + 2)
                    if tick < len(items) and items[tick]:
                        item_softmax(blk, items, tick)
                return walk.groups_after

            def token_exp_log():
                act.wait_ge(tok_ask, 1)
                chain(act.activation(fsp[:, 1, :, :], fsp[:, 1, :, :], ACT.Exp, scale=-1.0))
                act.activation(fsp[:, 1, :, :], fsp[:, 1, :, :], ACT.Ln, bias=1.0).then_inc(tok_answer, 1)

            def token_rsqrt(width):
                seen(ms_ready, "ms")
                rsqrt(width, 1.0)

            TOKEN_WORK_ACT = {1: {0: lambda: (token_rsqrt(4), token_exp_log())},
                              2: {0: lambda: token_rsqrt(20), 2: lambda: token_rsqrt(32)}}

            def turn_y(blk, tiles):
                for i in range(0, tiles, 2):
                    w = min(2, tiles - i)
                    seen(y_turned, "y_turned")
                    act.activation(yhi[:, i:i + w, :].rearrange("p a b -> p (a b)"), ps[:, (i // 2) % 4, 0:w * SEQ],
                                   ACT.Copy).then_inc(yhi_ready, 1)

            def up_and_out(l, blk, n0):
                for n in range(n0, n0 + 6):
                    split_high(l, blk, 1, n + 1)
                    split_high(l, blk, 0, n + 2)

            def gain_rows():
                for h in range(2):
                    seen(spread, "spread")
                    act.activation(gtb[:, h * 512:(h + 1) * 512], ps[:, 4 + h, :], ACT.Copy).then_inc(gain_copied, 1)

            act.preload_act_table_set("natural_log_exp_and_others")
            act.wait_ge(setup_in, 80)
            act.wait_ge(setup_chain, 1)
            act.activation(small[:, 16:24], csilu[:, :], ACT.Exp, scale=-1.0).then_inc(setup_chain, 1)
            act.wait_ge(setup_chain, 3)
            act.activation(rope2[:, :, :, :], rope2[:, :, :, :], ACT.Sin).then_inc(setup_chain, 1)
            act.preload_act_table_set("natural_log_exp_and_others")
            for blk in (1, 2):
                if blk == 2:
                    for t in range(NT):
                        act.activation(xn[:, t, :], x[:, t, :], ACT.Square, accum_out=ms[:, t:t + 1]).then_inc(between, 1)
                    act.wait_ge(between, 2)
                    act.activation(rs0[:, 0:NT], ms[:, 0:NT], ACT.Ln, scale=1.0 / D, bias=eps).then_inc(between, 1)
                    act.wait_ge(between, 3)
                    act.activation(rs0[:, 0:NT], rs0[:, 0:NT], ACT.Exp, scale=-0.5).then_inc(between, 1)
                    act.wait_ge(between, 10)
                with act.Fori(0, LAYERS) as l:
                    state.clear()
                    chain.n = 0
                    split_high(l, blk, 0, 0)
                    split_high(l, blk, 1, 0)
                    split_high(l, blk, 0, 1)
                    if blk == 1:
                        act.wait_ge(params_in, params_of(l, blk))
                        norm(lambda k: par[:, P1_G + k:P1_G + k + 1])
                        feed_forward(l, 1, 0, FF1, 2)
                        norm(lambda k: par[:, P1_G + 8 + k:P1_G + 9 + k])
                        done_groups = project_turned(l, 1, FF1)
                        done_groups = project_rows(l, 1, FF1 + 4, 4, 12, done_groups)
                        w = Walk(SLOTS1, FF1 + 8, 8, KD, done_groups)
                        ticks(l, 1, schedule1(), 24, w, FF1 + 8)
                        turn_y(1, YT1)
                        up_and_out(l, 1, FF1 + 16)
                        norm(lambda k: par[:, P1_G + 16 + k:P1_G + 17 + k])
                        feed_forward(l, 1, FF1 + 22, FF1, 2)
                    else:
                        act.wait_ge(params_in, params_of(l, blk))
                        act.wait_ge(mod_ready, 1)
                        norm(lambda k: ncol[:, k:k + 1], lambda k: mod[:, 0, k:k + 1])
                        gain_rows()
                        done_groups = project_rows(l, 2, 0, 6, 0, 0)
                        w = Walk(SLOTS2, 6, 6, KD, done_groups)
                        ticks(l, 2, schedule2(), 16, w, 6)
                        turn_y(2, YT2)
                        up_and_out(l, 2, 12)
                        norm(lambda k: ncol[:, KD + k:KD + k + 1], lambda k: mod[:, 0, 24 + k:25 + k])
                        gain_rows()
                        feed_forward(l, 2, 18, FF2, 1)
                    close_layer(act, l, blk)

        @block.vector
        def _(dve):
            chain = Count(dve, dve_chain)
            state = {}

            def seen(s, name, k=1):
                state[name] = state.get(name, 0) + k
                dve.wait_ge(s, state[name])

            def split_low(l, blk, kind, n, p=None, j=None, n0=None):
                slots = SL[blk]
                if j is None:
                    if n >= len(slots) or not slots[n][kind]:
                        return
                    p, width, count = n % 2, slots[n][kind] * P, parts_before(slots, kind, n + 1)
                else:
                    width, count = slots[n0][kind] * P, j + (parts_before(slots, kind, n0) + 1)
                dve.wait_ge(hi_ready[kind], count)
                dve.tensor_tensor(wlo[kind][:, p, 0:width], raw[kind][:, p, 0:width],
                                  whi[kind][:, p, 0:width].bitcast(F32), ALU.subtract).then_inc(lo_ready[kind], 1)

            def newton(width, scale):
                seen(guess_ready, "guess")
                w = slice(0, width)
                chain(dve.tensor_scalar(ms[:, w], ms[:, w], scale, EPS, ALU.mult, ALU.add))
                chain(dve.tensor_tensor(rt[:, w], rs0[:, w], rs0[:, w], ALU.mult))
                chain(dve.tensor_tensor(rt[:, w], rt[:, w], ms[:, w], ALU.mult))
                chain(dve.tensor_scalar(rt[:, w], rt[:, w], -0.5, 1.5, ALU.mult, ALU.add))
                chain(dve.tensor_tensor(rstd[:, w], rs0[:, w], rt[:, w], ALU.mult))

            def norm(cols, shifts=None):
                newton(NT, 1.0 / D)
                for t in range(NT):
                    dve.tensor_scalar(xn[:, t, :], x[:, t, :], rstd[:, t:t + 1], None, ALU.mult).then_inc(xn_ready, 1)
                for b in range(4):
                    seen(hhi_ready, "hhi")
                    for k in (2 * b, 2 * b + 1):
                        src = ps[:, b, (k % 2) * SEQ:(k % 2 + 1) * SEQ]
                        high = hhi[:, k, :].bitcast(F32)
                        if shifts is None:
                            m = dve.scalar_tensor_tensor(hlo[:, k, :], src, cols(k), high, ALU.mult, ALU.subtract)
                        else:
                            tmp = (fd, fq)[k % 2]
                            chain(dve.tensor_scalar(tmp[:, :], src, cols(k), shifts(k), ALU.mult, ALU.add))
                            m = dve.tensor_tensor(hlo[:, k, :], tmp[:, :], high, ALU.subtract)
                        if k % 2 == 0:
                            chain.also(m)
                    m.then_inc(hlo_ready, 1)

            def feed_forward(l, blk, n0, tiles, gates):
                e0 = state.get("ffn", 0)
                chain.per = 10 if gates == 2 else 4

                def step(j, p):
                    dve.wait_ge(exp_ready, j + (e0 + 1))
                    gated = fa if gates == 2 or p == 0 else fq
                    if gates == 2:
                        chain(dve.tensor_scalar(fd[:, :], ex[:, p, :], 1.0, None, ALU.add))
                        chain(dve.reciprocal(fd[:, :], fd[:, :]))
                        chain(dve.tensor_tensor(fq[:, :], ps[:, p, 0:SEQ], fd[:, :], ALU.mult))
                        chain(dve.tensor_tensor(fa[:, :], ps[:, p, SEQ:2 * SEQ], fq[:, :], ALU.mult))
                    else:
                        chain(dve.tensor_tensor(gated[:, :], ex[:, p, :], ex[:, p, :], ALU.mult))
                    chain(dve.tensor_copy(ghi[:, p, :], gated[:, :]))
                    dve.tensor_tensor(glo[:, p, :], gated[:, :], ghi[:, p, :].bitcast(F32),
                                      ALU.subtract).then_inc(gated_ready, 1)
                    if isinstance(j, int):
                        split_low(l, blk, 0, n0 + j + 2)
                        split_low(l, blk, 1, n0 + j + 1)
                    else:
                        split_low(l, blk, 0, None, p, j + 2, n0)
                        split_low(l, blk, 1, None, 1 - p, j + 1, n0)

                feed_forward_steps(dve, tiles, step, chain)
                state["ffn"] = e0 + tiles
                dve.wait_ge(used[1], parts_before(SL[blk], 1, n0 + tiles))
                for t in range(NT):
                    for h in range(2):
                        c = slice(h * 512, (h + 1) * 512)
                        if blk == 1:
                            dve.scalar_tensor_tensor(x[:, t, c], ps[:, 4 + 2 * t + h, :], 0.5, x[:, t, c],
                                                     ALU.mult, ALU.add).then_inc(x_ready, 1)
                        else:
                            gained_residual(t, h)

            def gained_residual(t, h):
                c = slice(h * 512, (h + 1) * 512)
                chain(dve.tensor_tensor(xn[:, t, c], ps[:, 4 + 2 * t + h, :], gtb[:, c], ALU.mult))
                dve.tensor_tensor(x[:, t, c], x[:, t, c], xn[:, t, c], ALU.add).then_inc(x_ready, 1)

            def gain_diagonals(g0):
                for h in range(2):
                    if h or g0 != 16:
                        seen(spread, "spread")
                    cols = mod[:, 0, g0 + 4 * h:g0 + 4 * h + 4]
                    dve.tensor_tensor(diag[:, :, :], ident.unsqueeze(1).broadcast_to([P, 4, P]),
                                      cols.unsqueeze(2).broadcast_to([P, 4, P]), ALU.mult).then_inc(diag_ready, 1)

            def projections(l, blk, n0, count):
                for n in range(n0, n0 + count):
                    split_low(l, blk, 1, n + 1)
                    split_low(l, blk, 0, n + 2)

            def item_early(blk, items, tick):
                kind, h = items[tick]
                s = (sm if blk == 1 else sm2)[:, tick % 2, :]
                bank = 2 + tick % 2
                if kind in HEADS:
                    e = count_upto(items, tick, lambda k: k in HEADS)
                    dve.wait_ge(scores_ready, e)
                    turned_before = heads_before(items, tick)
                    if turned_before:
                        dve.wait_ge(pt_ready, turned_before)
                    m = {"fox": mask(C_CAUSAL), "moba": mask(C_CAUSAL), "swa": mask(C_BAND), "sb": mask(C_STRICT),
                         "dsa": selmask[:, :]}[kind]
                    dve.tensor_tensor(s, ps[:, bank, 0:384], m, ALU.add).then_inc(scores_taken, 1)
                    dve.wait_ge(scores_taken, e)
                    if kind == "sb":
                        dve.scalar_tensor_tensor(aux[:, tick % 2, :], s, -1.0, s, ALU.mult, ALU.max).then_inc(abs_ready, 1)
                        return
                    chain.also(dve.tensor_reduce(rowmax[:, tick, 0:1], s[:, 0:P], AX.X, ALU.max, negate=True))
                    m = dve.tensor_reduce(rowmax[:, tick, 1:2], s[:, P:3 * P], AX.X, ALU.max, negate=True)
                    if kind == "swa":
                        chain(m)
                        m = dve.tensor_scalar(rowmax[:, tick, :], rowmax[:, tick, :], small[:, 32 + h:33 + h], None,
                                              ALU.min)
                    m.then_inc(max_ready, 1)
                elif kind == "idx":
                    dve.wait_ge(prep_copied, count_upto(items, tick, lambda k: k in PREP))
                    for t, c in ((0, slice(0, P)), (1, slice(P, 3 * P))):
                        base = consts[:, C_CHUNK + c.start:C_CHUNK + c.stop] if h == 0 else iscore[:, c]
                        m = dve.scalar_tensor_tensor(iscore[:, c], s[:, c], tok1[:, t, 1, 320 + h:321 + h], base,
                                                     ALU.mult, ALU.add)
                        if t == 0:
                            chain.also(m)
                    m.then_inc(index_added, 1)
                    dve.wait_ge(index_added, h + 1)
                    dve.wait_ge(dve_chain, chain.value())

            def item_late(blk, items, tick):
                kind, h = items[tick]
                if kind != "sb":
                    return
                s = sm[:, tick % 2, :]
                u = aux[:, tick % 2, :]
                dve.wait_ge(log_ready, count_upto(items, tick, lambda k: k == "sb"))
                chain(dve.scalar_tensor_tensor(u, s, 0.0, u, ALU.max, ALU.add))
                chain.also(dve.tensor_tensor_scan(run[:, 0:P][:, ::-1], u[:, 0:P][:, ::-1], u[:, 0:P][:, ::-1], 0.0,
                                                  ALU.add, ALU.bypass))
                chain(dve.tensor_tensor_scan(run[:, P:3 * P][:, ::-1], u[:, P:3 * P][:, ::-1], u[:, P:3 * P][:, ::-1],
                                             0.0, ALU.add, ALU.bypass))
                dve.tensor_tensor(s, s, run[:, :], ALU.subtract).then_inc(stick_ready, 1)

            def item_y(blk, items, tick):
                if tick < 0 or tick >= len(items) or not items[tick] or items[tick][0] not in HEADS:
                    return
                kind, h = items[tick]
                e = count_upto(items, tick, lambda k: k in HEADS)
                dve.wait_ge(pv_ready, e)
                y = y1 if blk == 1 else y2
                c = {"fox": 0, "sb": 384, "dsa": 768, "swa": 0, "moba": 512}[kind] + h * HD
                src = ps[:, 6 + e % 2, 0:P].rearrange("p (t d) -> p t d", t=NT)
                out = y[:, :, c:c + HD]
                if kind == "sb":
                    dve.tensor_copy(out, src).then_inc(y_done, 1)
                    return
                r = rowsum[:, tick, :]
                if kind == "swa":
                    chain(dve.tensor_tensor(r, r, sinkexp[:, tick, :], ALU.add))
                chain(dve.reciprocal(r, r))
                dve.tensor_tensor(out, src, r.unsqueeze(2).broadcast_to([P, NT, HD]), ALU.mult).then_inc(y_done, 1)

            def gate_sigmoid(blk, tick):
                g = (g1 if blk == 1 else g2)[:, tick, :]
                dve.wait_ge(gate_exp, tick + 1)
                chain(dve.tensor_scalar(g, g, 1.0, None, ALU.add))
                chain(dve.reciprocal(g, g))

            def ticks(l, blk, items, gates, n0):
                for tick in range(max(len(items) + 2, gates + 1)):
                    if tick < gates and tick % 3 == 0:
                        split_low(l, blk, 1, n0 + tick // 3 + 1)
                    if tick in TOKEN_WORK[blk]:
                        TOKEN_WORK[blk][tick]()
                    if tick < len(items) and items[tick]:
                        item_early(blk, items, tick)
                    item_y(blk, items, tick - 2)
                    if tick < len(items) and items[tick]:
                        item_late(blk, items, tick)
                    if tick < gates and (tick % 3 == 1 or (blk == 2 and tick == 15)):
                        split_low(l, blk, 0, n0 + tick // 3 + 2)
                    if 1 <= tick <= gates:
                        gate_sigmoid(blk, tick - 1)

            def rotate(x1, x2, cos, sin, tmp):
                chain.also(dve.tensor_tensor(tmp[0], x1, cos, ALU.mult))
                chain.also(dve.tensor_tensor(tmp[1], x2, sin, ALU.mult))
                chain.also(dve.tensor_tensor(tmp[2], x2, cos, ALU.mult))
                chain(dve.tensor_tensor(tmp[3], x1, sin, ALU.mult))
                chain.also(dve.tensor_tensor(x1, tmp[0], tmp[1], ALU.subtract))
                chain(dve.tensor_tensor(x2, tmp[2], tmp[3], ALU.add))

            def rotate1(v, heads):
                h = v.rearrange("p t (h d) -> p t h d", d=HD)
                r = consts[:, C_ROPE:C_ROPE + 32].rearrange("p (t c d) -> p t c d", t=NT, c=2)
                shape = [P, NT, heads, ROPE1]
                cos = r[:, :, 0, :].unsqueeze(2).broadcast_to(shape)
                sin = r[:, :, 1, :].unsqueeze(2).broadcast_to(shape)
                rotate(h[:, :, :, 0:ROPE1], h[:, :, :, ROPE1:2 * ROPE1], cos, sin,
                       [rope_tmp[:, i, :, 0:heads, :] for i in range(4)])

            def tokens1():
                dve.wait_ge(proj_copied, 28)
                for t in range(NT):
                    lat, key = tok1[:, t, 3, 0:P], tok1[:, t, 2, DSA * HD:DSA * HD + HD]
                    chain(dve.tensor_tensor(iscore[:, 0:P], lat, lat, ALU.mult))
                    chain(dve.tensor_reduce(ms[:, t:t + 1], iscore[:, 0:P], AX.X, ALU.add))
                    chain(dve.tensor_tensor(iscore[:, P:P + HD], key, key, ALU.mult))
                    chain(dve.tensor_reduce(ms[:, 2 + t:3 + t], iscore[:, P:P + HD], AX.X, ALU.add))
                chain(dve.tensor_scalar(ms[:, 0:2], ms[:, 0:2], 1.0 / P, None, ALU.mult))
                dve.tensor_scalar(ms[:, 2:4], ms[:, 2:4], 1.0 / HD, None, ALU.mult).then_inc(ms_ready, 1)
                bias = par[:, P1_BF:P1_BF + FOX].unsqueeze(1).broadcast_to([P, NT, FOX])
                chain(dve.tensor_tensor(fsp[:, 0, :, :], tok1[:, :, 1, 324:324 + FOX], bias, ALU.add))
                dve.scalar_tensor_tensor(fsp[:, 1, :, :], fsp[:, 0, :, :], -1.0, fsp[:, 0, :, :], ALU.mult,
                                         ALU.max).then_inc(tok_ask, 1)
                newton(4, 1.0)
                chain.also(dve.tensor_scalar(tok1[:, 0, 3, 0:P], tok1[:, 0, 3, 0:P], rstd[:, 0:1], None, ALU.mult))
                dve.tensor_scalar(tok1[:, 1, 3, 0:P], tok1[:, 1, 3, 0:P], rstd[:, 1:2], None,
                                  ALU.mult).then_inc(tokens_ready, 1)
                dve.wait_ge(tok_answer, 1)
                chain(dve.tensor_scalar(fsp[:, 2, :, :], fsp[:, 0, :, :], 0.0, None, ALU.min))
                chain(dve.tensor_tensor(fsp[:, 1, :, :], fsp[:, 1, :, :], fsp[:, 2, :, :], ALU.subtract))
                dve.tensor_copy(fcast[:, :, :, :],
                                fsp[:, 1, :, :].rearrange("p t h -> p h t").unsqueeze(3).broadcast_to(
                                    [P, FOX, NT, P])).then_inc(tokens_ready, 1)

            def tokens1_index():
                for t in range(NT):
                    key = tok1[:, t, 2, DSA * HD:DSA * HD + HD]
                    chain(dve.scalar_tensor_tensor(key, key, rstd[:, 2 + t:3 + t], par[:, P1_GIDX:P1_GIDX + HD],
                                                   ALU.mult, ALU.mult))
                rotate1(tok1[:, :, 2, DSA * HD:DSA * HD + HD], 1)
                for c in (0, HD):
                    chain.also(dve.tensor_copy(dup1[:, :, 0, c:c + HD], tok1[:, :, 2, DSA * HD:DSA * HD + HD]))
                rotate1(tok1[:, :, 3, P:P + IDX * HD], IDX)
                dve.drain().then_inc(tokens_ready, 1)

            def tokens1_queries():
                rotate1(tok1[:, :, 2, 0:DSA * HD], DSA)
                dve.drain().then_inc(tokens_ready, 1)

            def tokens1_latent():
                dve.wait_ge(prep_copied, 2)
                rotate1(kvv[:, :, 0:HD], 1)
                chain.also(dve.tensor_copy(dup1[:, :, 1, 0:HD], kvv[:, :, 0:HD]))
                dve.tensor_copy(dup1[:, :, 1, HD:2 * HD], kvv[:, :, 0:HD]).then_inc(tokens_ready, 1)

            def top_rounds(t, rounds):
                c = slice(0, P) if t == 0 else slice(P, 3 * P)
                for _ in range(rounds):
                    chain(dve.max(top8[:, :], iscore[:, c]))
                    chain(dve.match_replace(iscore[:, c], top8[:, :], iscore[:, c], PICKED))

            def finish_selection():
                chain(dve.tensor_scalar(selmask[:, :], iscore[:, :], PICKED / 2, MASKED, ALU.is_gt, ALU.mult))

            def tokens2_squares(c0, heads):
                for t in range(NT):
                    v = tok2[:, t, c0:c0 + heads * HD]
                    chain(dve.tensor_tensor(sq2[:, 0:heads * HD], v, v, ALU.mult))
                    chain(dve.tensor_reduce(ms[:, t * heads:(t + 1) * heads],
                                            sq2[:, 0:heads * HD].rearrange("p (h d) -> p h d", d=HD), AX.X, ALU.add))
                dve.tensor_scalar(ms[:, 0:NT * heads], ms[:, 0:NT * heads], 1.0 / HD, None,
                                  ALU.mult).then_inc(ms_ready, 1)

            def tokens2_rotate(c0, heads, groups):
                newton(NT * heads, 1.0)
                for t in range(NT):
                    v = tok2[:, t, c0:c0 + heads * HD].rearrange("p (h d) -> p h d", d=HD)
                    r = rstd[:, t * heads:(t + 1) * heads].unsqueeze(2).broadcast_to([P, heads, HD])
                    chain(dve.tensor_tensor(v, v, r, ALU.mult))
                    h0 = 0
                    for g, n in groups:
                        gain = par[:, P2_QK + g * HD:P2_QK + (g + 1) * HD].unsqueeze(1).broadcast_to([P, n, HD])
                        chain.also(dve.tensor_tensor(v[:, h0:h0 + n, :], v[:, h0:h0 + n, :], gain, ALU.mult))
                        h0 += n
                    dve.wait_ge(dve_chain, chain.value())
                    shape = [P, heads, ROPE2]
                    cos = rope2[:, t, 0, :].unsqueeze(1).broadcast_to(shape)
                    sin = rope2[:, t, 1, :].unsqueeze(1).broadcast_to(shape)
                    rotate(v[:, :, 0:ROPE2], v[:, :, ROPE2:HD], cos, sin,
                           [rope_tmp2[:, i, 0:heads * ROPE2].rearrange("p (h d) -> p h d", d=ROPE2) for i in range(4)])

            def tokens2_a():
                dve.wait_ge(proj_copied, 24)
                tokens2_squares(0, 10)

            def tokens2_a_rotate():
                tokens2_rotate(0, 10, [(0, SWA), (1, 2)])
                for g in range(2):
                    key = tok2[:, :, 512 + g * HD:512 + (g + 1) * HD]
                    chain.also(dve.tensor_copy(dup2[:, :, g, 0:HD], key))
                    chain.also(dve.tensor_copy(dup2[:, :, g, HD:2 * HD], key))
                dve.drain().then_inc(tokens_ready, 1)

            def tokens2_b_rotate():
                tokens2_rotate(768, 16, [(2, MOBA), (3, MOBA)])
                dve.drain().then_inc(tokens_ready, 1)

            TOKEN_WORK = {
                1: {0: tokens1, 1: tokens1_index, 2: tokens1_queries, 3: tokens1_latent,
                    10: lambda: top_rounds(0, 8), 11: lambda: top_rounds(1, 3), 12: lambda: top_rounds(1, 3),
                    13: lambda: (top_rounds(1, 2), finish_selection())},
                2: {0: tokens2_a, 1: tokens2_a_rotate, 2: lambda: tokens2_squares(768, 16), 3: tokens2_b_rotate}}

            def turn_y(tiles):
                for i in range(0, tiles, 2):
                    w = min(2, tiles - i)
                    seen(yhi_ready, "yhi")
                    dve.tensor_tensor(ylo[:, i:i + w, :].rearrange("p a b -> p (a b)"), ps[:, (i // 2) % 4, 0:w * SEQ],
                                      yhi[:, i:i + w, :].bitcast(F32).rearrange("p a b -> p (a b)"),
                                      ALU.subtract).then_inc(ylo_ready, 1)

            def merge(l, blk, walk, n0, branches, gt):
                g = g1 if blk == 1 else g2
                splits = [(k, n0 + i + d) for i in range(6) for k, d in ((1, 1), (0, 2))]

                def split_until(slot):
                    while splits and splits[0][1] <= slot + 1:
                        split_low(l, blk, *splits.pop(0))

                for f in range(KD):
                    last_slot = walk.tiles[(f + 1) * walk.group - 1][0]
                    split_until(last_slot)
                    sem_, val = walk.mark[f]
                    dve.wait_ge({"a": used[0], "b": used[1], "g": group_done}[sem_], val)
                    bank = 4 + 2 * (f % 2)
                    for br in range(branches):
                        chain.also(dve.tensor_tensor(mt[:, br, :], ps[:, bank + br // 2, (br % 2) * SEQ:(br % 2 + 1) * SEQ],
                                                     g[:, f * branches + br, :], ALU.mult))
                    dve.wait_ge(dve_chain, chain.value())
                    for br in range(1, branches):
                        chain(dve.tensor_tensor(mt[:, 0, :], mt[:, 0, :], mt[:, br, :], ALU.add))
                    chain(dve.tensor_copy(hhi[:, f, :], mt[:, 0, :]))
                    dve.tensor_tensor(hlo[:, f, :], mt[:, 0, :], hhi[:, f, :].bitcast(F32),
                                      ALU.subtract).then_inc(merged_ready, 1)
                    dve.wait_ge(merged_ready, f + 1)
                while splits:
                    split_low(l, blk, *splits.pop(0))
                dve.wait_ge(used[0], parts_before(SL[blk], 0, n0 + 6))
                if gt:
                    seen(gain_copied, "gain", 2)
                for t in range(NT):
                    for h in range(2):
                        c = slice(h * 512, (h + 1) * 512)
                        if gt:
                            gained_residual(t, h)
                        else:
                            dve.tensor_tensor(x[:, t, c], ps[:, 4 + 2 * t + h, :], x[:, t, c],
                                              ALU.add).then_inc(x_ready, 1)

            def ada(l, blk):
                for c in range(12):
                    dve.wait_ge(ada_in[c % 2], l * 96 + 16 * (c // 2 + 1))
                    if c >= 2:
                        dve.wait_ge(ada_used, c - 1)
                    acc = ada_acc[:, c % 2, :]
                    for k in range(KD):
                        w = ada_w[:, c % 2, k, :]
                        if k == 0:
                            m = dve.tensor_scalar(acc, w, csilu[:, 0:1], None, ALU.mult)
                        else:
                            m = dve.scalar_tensor_tensor(acc, w, csilu[:, k:k + 1], acc, ALU.mult, ALU.add)
                        if k < KD - 1:
                            chain(m)
                    m.then_inc(ada_sum, 1)
                dve.wait_ge(ada_used, 12)
                dve.wait_ge(params_in, params_of(l, blk))
                chain(dve.tensor_tensor(mod[:, 0, :], ps[:, 7, 0:48], par[:, P2_BADA:P2_BADA + 48], ALU.add))
                chain(dve.tensor_scalar(small[:, 32:40], par[:, P2_SINK:P2_SINK + SWA], -1.0, None, ALU.mult))
                chain(dve.scalar_tensor_tensor(ncol[:, 0:KD], mod[:, 0, 8:16], 1.0, par[:, P2_G:P2_G + 8],
                                               ALU.add, ALU.mult))
                dve.scalar_tensor_tensor(ncol[:, KD:2 * KD], mod[:, 0, 32:40], 1.0, par[:, P2_G + 8:P2_G + 16],
                                         ALU.add, ALU.mult).then_inc(mod_ready, 1)
                dve.wait_ge(mod_ready, 1)

            own = Count(dve, setup_vector)
            own(dve.memset(small[:, 60:61], EPS))
            dve.wait_ge(setup_in, 80)
            dve.memset(small[:, 62:63], 0.0).then_inc(setup_chain, 1)
            dve.wait_ge(setup_chain, 2)
            own(dve.tensor_scalar(small[:, 16:24], small[:, 16:24], 1.0, None, ALU.add))
            own(dve.reciprocal(small[:, 16:24], small[:, 16:24]))
            own(dve.tensor_tensor(csilu[:, :], csilu[:, :], small[:, 16:24], ALU.mult))
            own(dve.tensor_copy(small[:, 4:4 + NT], small[:, 0:NT].bitcast(I32)))
            turns = small[:, 24:25]
            ang, k_, tmp = sm2[:, 0, 0:ROPE2], sm2[:, 0, 64:64 + ROPE2], sm2[:, 0, 128:128 + ROPE2]
            for t in range(NT):
                for i, quarter in ((0, 0.25), (1, 0.0)):
                    own(dve.tensor_scalar(ang, consts[:, C_INVF:C_INVF + ROPE2], small[:, 4 + t:5 + t], None, ALU.mult))
                    own(dve.tensor_scalar(k_, ang, 1.0 / (2 * np.pi), quarter, ALU.mult, ALU.add))
                    own(dve.tensor_scalar(k_, k_, 12582912.0, None, ALU.add))
                    own(dve.tensor_scalar(k_, k_, 12582912.0, None, ALU.subtract))
                    for part in TWO_PI:
                        own(dve.tensor_scalar(tmp, k_, part, None, ALU.mult))
                        own(dve.tensor_tensor(ang, ang, tmp, ALU.subtract))
                    own(dve.tensor_scalar(ang, ang, quarter * 2 * np.pi, None, ALU.add))
                    own(dve.tensor_scalar(rope2[:, t, i, :], ang, 3.1415925, -3.1415925, ALU.min, ALU.max))
            dve.memset(small[:, 62:63], 0.0).then_inc(setup_chain, 1)

            for blk in (1, 2):
                if blk == 2:
                    dve.wait_ge(setup_chain, 4)
                    dve.wait_ge(between, 4)
                    last_norm = Count(dve, between)
                    last_norm.n = 4
                    w = slice(0, NT)
                    last_norm(dve.tensor_scalar(ms[:, w], ms[:, w], 1.0 / D, EPS, ALU.mult, ALU.add))
                    last_norm(dve.tensor_tensor(rt[:, w], rs0[:, w], rs0[:, w], ALU.mult))
                    last_norm(dve.tensor_tensor(rt[:, w], rt[:, w], ms[:, w], ALU.mult))
                    last_norm(dve.tensor_scalar(rt[:, w], rt[:, w], -0.5, 1.5, ALU.mult, ALU.add))
                    last_norm(dve.tensor_tensor(rstd[:, w], rs0[:, w], rt[:, w], ALU.mult))
                    for t in range(NT):
                        last_norm(dve.scalar_tensor_tensor(x[:, t, :], x[:, t, :], rstd[:, t:t + 1], gfin[:, :],
                                                           ALU.mult, ALU.mult))
                with dve.Fori(0, LAYERS) as l:
                    state.clear()
                    chain.n = 0
                    dve.sem_inc(x_ready, 4)
                    state["x"] = 4
                    split_low(l, blk, 0, 0)
                    split_low(l, blk, 1, 0)
                    split_low(l, blk, 0, 1)
                    if blk == 1:
                        g = lambda k: par[:, P1_G + k:P1_G + k + 1]
                        norm(g)
                        feed_forward(l, 1, 0, FF1, 2)
                        norm(lambda k: g(8 + k))
                        projections(l, 1, FF1, 8)
                        chain(dve.memset(y1[:, :, 384 + SB * HD:768], 0.0))
                        chain(dve.memset(y1[:, :, 768 + DSA * HD:YT1 * P], 0.0))
                        ticks(l, 1, schedule1(), 24, FF1 + 8)
                        turn_y(YT1)
                        merge(l, 1, Walk(SLOTS1, FF1 + 16, 3, YT1, G_AT[1]), FF1 + 16, 3, False)
                        norm(lambda k: g(16 + k))
                        feed_forward(l, 1, FF1 + 22, FF1, 2)
                    else:
                        ada(l, blk)
                        norm(lambda k: ncol[:, k:k + 1], lambda k: mod[:, 0, k:k + 1])
                        gain_diagonals(16)
                        projections(l, 2, 0, 6)
                        ticks(l, 2, schedule2(), 16, 6)
                        turn_y(YT2)
                        merge(l, 2, Walk(SLOTS2, 12, 3, YT2, G_AT[2]), 12, 2, True)
                        norm(lambda k: ncol[:, KD + k:KD + k + 1], lambda k: mod[:, 0, 24 + k:25 + k])
                        gain_diagonals(40)
                        seen(gain_copied, "gain", 2)
                        feed_forward(l, 2, 18, FF2, 1)
                    close_layer(dve, l, blk)


def lay_out(inputs):
    a = {}

    def tiles(w, cols):
        n_l, k, n = w.shape
        return w.reshape(n_l, k // P, P, n // cols, cols).transpose(0, 3, 2, 1, 4)

    def pad(w, rows=None, cols=None):
        out = np.zeros((w.shape[0], rows or w.shape[1], cols or w.shape[2]), w.dtype)
        out[:, :w.shape[1], :w.shape[2]] = w
        return out

    def parts(name, stream, count):
        n_l = stream.shape[0]
        full = np.zeros((n_l, count * 24, P, P), stream.dtype)
        full[:, :stream.shape[1]] = stream
        full = full.reshape(n_l, count, 24, P, P).transpose(0, 1, 3, 2, 4)
        a[name + "_a"] = full[:, :, :, :16].reshape(n_l, count, P, 16 * P)
        a[name + "_b"] = full[:, :, :, 16:].reshape(n_l, count, P, 8 * P)

    def as_tiles(w):
        n_l, k, n = w.shape
        return w.reshape(n_l, k // P, P, n // P, P).transpose(0, 3, 1, 2, 4)

    for name, gu, down in (("w1_ffn_a", "w_ffn1_gu", "w_ffn1_down"), ("w1_ffn_b", "w_ffn2_gu", "w_ffn2_down")):
        t = as_tiles(inputs[gu])
        both = np.concatenate([t[:, :FF1], t[:, FF1:]], axis=2)
        a[name + "_a"] = both.transpose(0, 1, 3, 2, 4).reshape(LAYERS, FF1, P, 16 * P)
        a[name + "_b"] = inputs[down].reshape(LAYERS, FF1, P, D)
    t = as_tiles(inputs["w_up_2"])
    a["w2_ffn_a"] = t.transpose(0, 1, 3, 2, 4).reshape(LAYERS, FF2, P, 8 * P)
    a["w2_ffn_b"] = inputs["w_down_2"].reshape(LAYERS, FF2, P, D)

    w, at, cut = inputs["w_in"], 0, {}
    for key, n in (("qa", 384), ("ka", 384), ("va", 384), ("fa", FOX), ("qb", 320), ("kb", 320), ("vb", 320),
                   ("qc", 320), ("ckv", 128), ("qi", 256), ("ki", 64), ("wi", IDX), ("gates", 3 * D)):
        cut[key] = w[:, :, at:at + n]
        at += n
    groups = [("qa",), ("ka",), ("qb",), ("kb",), ("va",), ("vb", "wi", "fa"), ("qc", "ki"), ("ckv", "qi")]
    slots = np.stack([pad(np.concatenate([cut[k] for k in g], axis=2), cols=384) for g in groups], axis=1)

    def row_parts(name, slots):
        n_l, n = slots.shape[:2]
        s = slots.reshape(n_l, n, KD, P, 384).transpose(0, 1, 3, 2, 4)
        a[name + "_a"] = s[..., :256].reshape(n_l, n, P, KD * 256)
        a[name + "_b"] = s[..., 256:].reshape(n_l, n, P, KD * P)

    row_parts("w1_proj", slots)
    g = as_tiles(cut["gates"]).reshape(LAYERS, 3, KD, KD, P, P).transpose(0, 2, 1, 3, 4, 5)
    parts("w1_gate", g.reshape(LAYERS, 192, P, P), 8)
    up = np.concatenate([pad(inputs["w_up_fox"], rows=384), pad(inputs["w_up_sb"], rows=384),
                         pad(inputs["w_up_dsa"], rows=384)], axis=1)
    parts("w1_up", as_tiles(up).reshape(LAYERS, 72, P, P), 3)

    def out_parts(name, w):
        parts(name, w.reshape(LAYERS, KD, P, KD, P).transpose(0, 1, 3, 2, 4).reshape(LAYERS, 64, P, P), 3)

    out_parts("w1_out", inputs["w_out"])
    out_parts("w2_out", inputs["w_out_2"])
    w = inputs["w_in_2"]
    row_parts("w2_proj", w[:, :, :W_IN2].reshape(LAYERS, D, 6, 384).transpose(0, 2, 1, 3))
    g = as_tiles(w[:, :, W_IN2:]).reshape(LAYERS, 2, KD, KD, P, P).transpose(0, 2, 1, 3, 4, 5)
    parts("w2_gate", g.reshape(LAYERS, 128, P, P), 6)
    up = np.concatenate([inputs["w_o_swa_2"], inputs["w_o_moba_2"]], axis=1)
    parts("w2_up", as_tiles(up).reshape(LAYERS, 64, P, P), 3)
    a["w2_ada"] = tiles(inputs["w_ada_2"], 512)

    def cols(v):
        return v.reshape(v.shape[0], -1, P).transpose(0, 2, 1)

    def rows(v):
        return np.broadcast_to(v[:, None, :], (v.shape[0], P, v.shape[1]))

    a["params1"] = np.concatenate([cols(inputs["g_ffn1"]), cols(inputs["g_mix"]), cols(inputs["g_ffn2"]),
                                   cols(inputs["g_kv_latent"]), rows(inputs["b_forget"]), rows(inputs["g_idx_k"]),
                                   inputs["w_kv_up"]], axis=2)
    a["params2"] = np.concatenate([cols(inputs["rms_mix_2"]), cols(inputs["rms_mlp_2"]), cols(inputs["b_ada_2"]),
                                   rows(inputs["q_norm_swa_2"]), rows(inputs["k_norm_swa_2"]),
                                   rows(inputs["q_norm_moba_2"]), rows(inputs["k_norm_moba_2"]),
                                   rows(inputs["swa_sinks_2"])], axis=2)
    a["x"] = inputs["x"].reshape(SEQ, D)
    a["g_final"] = np.broadcast_to(inputs["g_final"], (P, D))
    a["c"] = inputs["c_2"].reshape(KD, P).T
    a["positions"] = inputs["positions_2"].reshape(NT, P).T
    return a


def shape_constants():
    f = np.float32
    q, k = np.arange(P)[:, None], np.arange(P)[None, :]
    zero, full = np.zeros((P, P), f), np.full((P, P), MASKED, f)
    causal = np.where(k <= q, 0, MASKED).astype(f)
    strict = np.where(k < q, 0, MASKED).astype(f)
    beyond = np.where(k > q, 0, MASKED).astype(f)
    assert WINDOW == P
    chunk = np.where(k // CHUNK <= q // CHUNK, 0, MASKED).astype(f)
    upper = (q <= k).astype(f)
    inv = (f(500000.0) ** (-np.arange(0, 16, 2, dtype=f) / f(16))).astype(f)
    ang = np.arange(SEQ, dtype=f)[:, None] * inv[None, :]
    rope = np.stack([np.cos(ang), np.sin(ang)], axis=1).reshape(NT, P, 2 * ROPE1).transpose(1, 0, 2).reshape(P, 32)
    inv2 = (f(10000.0) ** (-np.arange(ROPE2, dtype=f) / f(ROPE2))).astype(f)
    out = np.concatenate([np.eye(P, dtype=f), causal, zero, causal, strict, zero, strict, chunk, zero, chunk,
                          causal, beyond, causal, upper, np.ones((P, P), f), rope.astype(f),
                          np.broadcast_to(inv2, (P, ROPE2))], axis=1)
    assert out.shape == (P, C_END)
    return np.ascontiguousarray(out, dtype=f)


def kernel(**inputs):
    import numpy as _np
    import concourse.bacc as _bacc
    from concourse import mybir as _mybir
    from concourse.bass_utils import run_bass_kernel_spmd as _run

    nc = _bacc.Bacc("TRN2", target_bir_lowering=False, num_devices=1)
    laid = lay_out({k: _np.asarray(v) for k, v in inputs.items()})
    laid["consts"] = shape_constants()
    arrays, aps = {}, {}
    for name, v in laid.items():
        v = _np.ascontiguousarray(v)
        arrays[f"in_{name}"] = v
        aps[name] = nc.dram_tensor(f"in_{name}", v.shape, _mybir.dt.from_np(v.dtype), kind="ExternalInput").ap()
    aps["out"] = nc.dram_tensor("out_0", (SEQ, D), _mybir.dt.float32, kind="ExternalOutput").ap()
    build(nc, aps)
    r = _run(nc, [arrays], core_ids=[0])
    return r.results[0]["out_0"].reshape(1, SEQ, D)
```

```python
from contextlib import ExitStack

import numpy as np

import concourse.bass as bass
from concourse import mybir

ALU = mybir.AluOpType
ACT = mybir.ActivationFunctionType
AX = mybir.AxisListType
F32 = mybir.dt.float32
F32R = mybir.dt.float32r
I32 = mybir.dt.int32

P = 128
SEQ, D, LAYERS = 256, 1024, 2
NT = SEQ // P
KD = D // P
HD = 64
EPS = 1e-6
SCALE = HD ** -0.5
MASKED = -1e30
PICKED = -3e38
TOPK = min(256, SEQ // 4)
CHUNK = 64
WINDOW = 128

FF1 = 2816 // P
FOX, SB, DSA, IDX = 6, 5, 5, 4
ROPE1 = 8
BRANCH1, BRANCH2 = 3, 2
YT1 = 9
FF2 = 4096 // P
SWA, MOBA = 8, 8
ROPE2 = 32
W_IN2 = 2304
YT2 = 8

TA, TB = 16, 8
PROJ1 = [(16, 8)] * 8
GATE1 = [(16, 8)] * 8
UP1 = [(16, 8)] * 3
OUT = [(16, 8), (16, 8), (16, 0)]
PROJ2 = [(16, 8)] * 6
GATE2 = [(16, 8)] * 5 + [(8, 0)]
UP2 = [(16, 8), (16, 8), (16, 0)]
SLOTS1 = [(16, 8)] * FF1 + PROJ1 + GATE1 + UP1 + OUT + [(16, 8)] * FF1
SLOTS2 = PROJ2 + GATE2 + UP2 + OUT + [(8, 8)] * FF2
assert len(SLOTS1) % 2 == 0 and len(SLOTS2) % 2 == 0

UP_BANKS = (4, 6, 0, 2)

P1_G, P1_GKV, P1_BF, P1_GIDX, P1_WKV, P1_END = 0, 24, 25, 31, 95, 223
P2_G, P2_BADA, P2_QK, P2_SINK, P2_END = 0, 16, 64, 320, 328
ADA, MOD = 384, 6 * KD
ADA_CHUNKS = 6 * D // ADA // 2
C_ID, C_CAUSAL, C_STRICT, C_CHUNK, C_BAND, C_U, C_ROPE, C_INVF, C_END = (
    0, 128, 512, 896, 1280, 1664, 1920, 1952, 1984)
TWO_PI = (6.28125, 0.0019350051879882812, 3.0199159819567e-07)


def parts_before(slots, kind, n):
    return sum(1 for s in slots[:n] if s[kind])


class Walk:

    def __init__(self, slots, n0, count, group, groups_before):
        self.tiles = [(n, kind, i, i == slots[n][kind] - 1)
                      for n in range(n0, n0 + count) for kind in (0, 1) for i in range(slots[n][kind])]
        self.group = group
        self.mark = []
        g = groups_before
        for e in range(group - 1, len(self.tiles), group):
            n, kind, _, end = self.tiles[e]
            if end:
                self.mark.append(("ab"[kind], parts_before(slots, kind, n + 1)))
            else:
                g += 1
                self.mark.append(("g", g))
        self.groups_after = g


class Count:

    def __init__(self, eng, sem):
        self.eng, self.sem, self.n, self.loop = eng, sem, 0, None

    def value(self):
        return self.n if self.loop is None else self.loop + self.n

    def __call__(self, ins):
        ins.then_inc(self.sem, 1)
        self.n += 1
        self.eng.wait_ge(self.sem, self.value())

    def behind(self):
        self.eng.wait_ge(self.sem, self.value() - 1)

    def also(self, ins):
        ins.then_inc(self.sem, 1)
        self.n += 1


def feed_forward_steps(eng, tiles, step, chain=None):
    for j in range(3):
        step(j, j % 2, None)
    turns = (tiles - 7) // 2
    before = chain.n if chain else 0
    per = chain.per if chain else 0
    with eng.Fori(0, turns) as i:
        if chain:
            chain.loop = i * per
        for u in range(2):
            step(i * 2 + 3 + u, (3 + u) % 2, i)
    if chain:
        assert chain.n - before == per, (chain.n - before, per)
        chain.loop = None
        chain.n = before + per * turns
    for j in range(3 + 2 * turns, tiles):
        step(j, j % 2, None)


assert (FF1 - 7) // 2 == ADA_CHUNKS - 1


def schedule1():
    items = [("ckv", 0), ("fox", 0), ("kv", 0), ("fox", 1), ("turn", 0), ("turn", 1)]
    items += [("idx", h) for h in range(IDX)]
    items += [("turn", 2), ("turn", 3)]
    items += [("fox", h) for h in range(2, FOX)]
    items += [("sb", h) for h in range(SB)] + [("dsa", h) for h in range(DSA)]
    return items


def schedule2():
    items = [("turn", 0), ("turn", 1), ("swa", 0), ("swa", 1), ("turn", 2)]
    items += [("swa", h) for h in range(2, SWA)] + [("turn", h) for h in range(3, 7)]
    items += [("moba", h) for h in range(MOBA)]
    return items


HEADS = ("fox", "sb", "dsa", "swa", "moba")
READ_BY = {"fox": "scores_taken", "sb": "scores_taken", "dsa": "scores_taken", "swa": "scores_taken",
           "moba": "scores_taken", "idx": "prep_copied", "ckv": "prep_copied", "kv": "prep_copied",
           "turn": "prep_copied"}


def heads_before(items, tick):
    back = [i for i in range(tick % 3, tick, 3) if items[i] and items[i][0] in HEADS]
    return count_upto(items, back[-1], lambda k: k in HEADS) if back else 0


def count_upto(items, tick, what):
    return sum(1 for x in items[:tick + 1] if x and what(x[0]))


def build(nc, a):
    with ExitStack() as ctx:
        start = 16512
        at = [start]

        def put(name, shape, dt=F32, where=None):
            size = int(np.prod(shape[1:])) * 4
            off = at[0] if where is None else where
            t = nc.alloc_sbuf_tensor_at(name, shape, dt, offset=off)
            if where is None:
                at[0] = off + (size + 31) // 32 * 32
            return t

        raw = [put(f"raw_{'ab'[k]}", [P, 2, (TA, TB)[k] * P]) for k in range(2)]
        whi = [put(f"weights_high_{'ab'[k]}", [P, 2, (TA, TB)[k] * P], F32R) for k in range(2)]
        wlo = [put(f"weights_low_{'ab'[k]}", [P, 2, (TA, TB)[k] * P], F32R) for k in range(2)]
        x = put("residual", [P, NT, D])
        hhi = put("h_high", [P, KD, SEQ], F32R)
        hlo = put("h_low", [P, KD, SEQ], F32R)
        consts = put("constants", [P, C_END])
        par = put("layer_parameters", [P, max(P1_END, P2_END)])
        small = put("small", [P, 64])
        ms = put("mean_squares", [P, 64])
        rs0 = put("rsqrt_guess", [P, 64])
        rt = put("rsqrt_temp", [P, 64])
        rstd = put("rstd", [P, 64])
        rowmax = put("negated_row_max", [P, 32, NT])
        rowsum = put("row_sums", [P, 32, NT])
        sinkexp = put("sink_exps", [P, 32, NT])
        csilu = put("silu_c", [P, KD])
        half_ms = put("half_mean_squares", [P, NT])
        mod_raw = put("modulation_sums", [P, LAYERS * MOD])
        mod = put("modulation_columns", [P, MOD])
        ncol = put("norm_columns", [P, 2 * KD])
        angle_temp = put("angle_temps", [P, 2, NT, 2, ROPE2])
        rope2 = put("rope_tables_two", [P, NT, 2, ROPE2])
        ones_r = put("column_of_ones", [P, 2], F32R)
        mid = at[0]

        xn = put("x_normed", [P, NT, D], F32, mid)
        scaled_id = put("identity_by_rstd", [P, NT, P], F32, mid + 8192)
        ex = put("gate_activation", [P, 2, SEQ], F32, mid + 8192)
        fd = put("modulated", [P, SEQ], F32, mid + 10240)
        fq = put("gate_part", [P, SEQ], F32, mid + 11264)
        fa = put("gated", [P, SEQ], F32, mid + 12288)
        ghi = put("gated_high", [P, 2, SEQ], F32R, mid + 13312)
        glo = put("gated_low", [P, 2, SEQ], F32R, mid + 15360)
        ada_w = put("ada_weights", [P, 2, KD // 2, ADA], F32, mid + 17408)
        ada_acc = put("ada_sums", [P, ADA_CHUNKS * ADA], F32, mid + 17408 + KD * ADA * 4)
        ada_hi = put("ada_sums_high", [P, ADA_CHUNKS * ADA], F32R, mid + 17408 + (KD + ADA_CHUNKS) * ADA * 4)
        ada_lo = put("ada_sums_low", [P, ADA_CHUNKS * ADA], F32R, mid + 17408 + (KD + 2 * ADA_CHUNKS) * ADA * 4)
        at[0] = mid
        tok1 = put("tokens_one", [P, NT, 4, 384])
        qk1 = put("q_k_turned_one", [P, 4, 3, SEQ])
        g1 = put("gates_one", [P, 24, SEQ])
        y1 = put("y_one", [P, NT, YT1 * P])
        tt1 = put("turned_one", [P, 7, SEQ])
        dup1 = put("index_and_latent_keys", [P, NT, 2, P])
        kvt = put("latent_turned", [P, SEQ])
        kvv = put("latent_k_v", [P, NT, P])
        fsp = put("forget_softplus", [P, 3, NT, FOX])
        fcast = put("forget_cast", [P, FOX, NT, P])
        iscore = put("index_scores", [P, 384])
        selmask = put("selection_mask", [P, 384])
        top8 = put("top_eight", [P, 8])
        sm = put("scores", [P, 3, 384])
        aux = put("softplus", [P, 2, 384])
        run = put("stick_sums", [P, 384])
        pts = put("probs_turned", [P, 2, 384])
        rope_tmp = put("rope_temp", [P, 4, NT, 5, ROPE1])
        end1 = at[0]
        at[0] = mid
        tok2 = put("tokens_two", [P, NT, W_IN2])
        tt2 = put("turned_two", [P, 14, SEQ])
        g2 = put("gates_two", [P, 16, SEQ])
        y2 = put("y_two", [P, NT, YT2 * P])
        dup2 = put("window_keys_doubled", [P, NT, 2, P])
        sm2 = put("scores_two", [P, 3, 384])
        pts2 = put("probs_turned_two", [P, 2, 384])
        rope_tmp2 = put("rope_temp_two", [P, 4, 16 * ROPE2])
        sq2 = put("squares_two", [P, 1024])
        diag = put("gain_diagonals", [P, 4, P])
        end2 = at[0]
        gtb = put("residual_gain", [P, D], F32, max(end1, end2))
        gfin = put("final_gain", [P, D], F32, max(end1, end2) + 4096)
        assert mid + 17408 + (KD + 3 * ADA_CHUNKS) * ADA * 4 <= max(end1, end2)
        assert max(end1, end2) + 8192 <= nc.sbuf_usable_end, (end1, end2)
        yhi = put("y_high", [P, YT1, SEQ], F32R, mid)
        ylo = put("y_low", [P, YT1, SEQ], F32R, mid + YT1 * SEQ * 4)
        mt = put("merge_terms", [P, 3, SEQ], F32, end2 - 3 * SEQ * 4 if end2 > end1 else end1 - 3 * SEQ * 4)

        ident = consts[:, C_ID:C_ID + P]
        ones = consts[:, C_U + P:C_U + 2 * P]

        def mask(c):
            return consts[:, c:c + 384]

        ps = ctx.enter_context(nc.psum_tensor("psum", [P, 8, 512], F32))

        def sem(name):
            return ctx.enter_context(nc.semaphore(name))

        land = [[sem(f"landed_{k}{u}") for u in range(2)] for k in "ab"]
        lo_ready = [sem("low_a_ready"), sem("low_b_ready")]
        layer_done, layer_open = sem("layer_done"), sem("layer_open")
        between, layers_closed = sem("between_blocks"), sem("layers_closed")
        params_in, ada_in = sem("params_in"), [sem("ada_in_0"), sem("ada_in_1")]
        small_in, x_in, consts_in = sem("small_in"), sem("x_in"), sem("constants_in")
        final_gain_in, out_done = sem("final_gain_in"), sem("out_done")
        angles_ready, tables_ready = sem("angles_ready"), sem("tables_ready")
        setup_chain, setup_vector = sem("setup_chain"), sem("setup_vector")
        first = sem("ada_half_0")
        ada_half = [first, sem("ada_half_1")]
        hi_ready = [sem("high_a_ready"), sem("high_b_ready")]
        used = [sem("used_a"), sem("used_b")]
        group_done = sem("group_done")
        act_ready, gated_ready = sem("activation_ready"), sem("gated_ready")
        x_ready, guess_ready, scale_ready = sem("x_ready"), sem("guess_ready"), sem("scale_ready")
        ms_ready, squares_ready = sem("ms_ready"), sem("squares_ready")
        turned, hhi_ready, hlo_ready = sem("turned"), sem("h_high_ready"), sem("h_low_ready")
        proj_copied = sem("proj_copied")
        scores_ready, scores_taken = sem("scores_ready"), sem("scores_taken")
        max_ready, probs_ready = sem("max_ready"), sem("probs_ready")
        abs_ready, log_ready, stick_ready = sem("abs_ready"), sem("log_ready"), sem("stick_ready")
        pt_ready, pt_copied, pv_ready, y_done = sem("pt_ready"), sem("pt_copied"), sem("pv_ready"), sem("y_done")
        prep_ready, prep_copied = sem("prep_ready"), sem("prep_copied")
        tokens_ready, index_added = sem("tokens_ready"), sem("index_added")
        tok_ask, tok_answer = sem("tokens_ask"), sem("tokens_answer")
        gate_copied, gates_ready = sem("gate_copied"), sem("gates_ready")
        merged_ready, sums_ready = sem("merged_ready"), sem("sums_ready")
        y_turned, yhi_ready, ylo_ready = sem("y_turned"), sem("y_high_ready"), sem("y_low_ready")
        ada_used, ada_copied = sem("ada_used"), sem("ada_copied")
        ada_hi_ready, ada_lo_ready = sem("ada_high_ready"), sem("ada_low_ready")
        mod_ready = sem("mod_ready")
        diag_ready, spread, gain_copied = sem("diag_ready"), sem("spread"), sem("gain_copied")
        dve_chain, act_chain = sem("vector_chain"), sem("scalar_chain")
        last = act_chain
        cleared = range(first.num, last.num + 1)

        block = ctx.enter_context(nc.Block())

        segments = {
            1: [("ffn_a", FF1), ("proj", 8), ("gate", 8), ("up", 3), ("out", 3), ("ffn_b", FF1)],
            2: [("proj", 6), ("gate", 6), ("up", 3), ("out", 3), ("ffn", FF2)],
        }
        SL = {1: SLOTS1, 2: SLOTS2}

        def landed_before(blk, kind, parity):
            return LAYERS * sum(1 for n, s in enumerate(SLOTS1) if s[kind] and n % 2 == parity) if blk == 2 else 0

        def per_layer(blk, kind, parity):
            return sum(1 for n, s in enumerate(SL[blk]) if s[kind] and n % 2 == parity)

        def lo_before(blk, kind):
            return LAYERS * parts_before(SLOTS1, kind, len(SLOTS1)) if blk == 2 else 0

        @block.sync
        def _(sp):
            sp.dma_start(csilu[:, :], a["c"]).then_inc(small_in, 16)
            sp.dma_start(small[:, 0:NT].bitcast(I32), a["positions"]).then_inc(small_in, 16)
            sp.dma_start(x[:, :, :], a["x"].rearrange("(t p) d -> p t d", p=P)).then_inc(x_in, 16)
            sp.dma_start(consts[:, :], a["consts"]).then_inc(consts_in, 16)
            sp.dma_start(gfin[:, :], a["g_final"]).then_inc(final_gain_in, 16)
            for blk in (1, 2):
                slots = SL[blk]
                with sp.Fori(0, LAYERS) as l:
                    n0 = 0
                    for name, count in segments[blk]:
                        def load(j, p, n0=n0, name=name):
                            static = isinstance(j, int)
                            for kind in (0, 1):
                                tiles = slots[n0 + j][kind] if static else slots[n0][kind]
                                if not tiles:
                                    continue
                                if not static:
                                    before = parts_before(slots, kind, n0) + j - 1
                                else:
                                    before = parts_before(slots, kind, n0 + j - 1) if n0 + j else -1
                                sp.wait_ge(lo_ready[kind], l * parts_before(slots, kind, len(slots))
                                           + before + (lo_before(blk, kind) + 2))
                                src = a[f"w{blk}_{name}_{'ab'[kind]}"]
                                sp.dma_start(raw[kind][:, p, 0:tiles * P],
                                             src[l, j, :, 0:tiles * P]).then_inc(land[kind][p], 16)

                        if name.startswith("ffn"):
                            load(0, n0 % 2)
                            load(1, (n0 + 1) % 2)
                            with sp.Fori(0, count // 2 - 1) as i:
                                for u in range(2):
                                    load(i * 2 + 2 + u, (n0 + u) % 2)
                        else:
                            for j in range(count):
                                load(j, (n0 + j) % 2)
                        n0 += count
            sp.wait_ge(layer_done, 3 * LAYERS * 2)
            sp.dma_start(a["out"].rearrange("(t p) d -> p t d", p=P), x[:, :, :]).then_inc(out_done, 16)
            sp.wait_ge(out_done, 16)

        @block.gpsimd
        def _(pool):
            pool.sem_inc(lo_ready[0], 2)
            pool.sem_inc(lo_ready[1], 2)

            def ada_loads(l, f):
                for h in range(2):
                    pool.dma_start(ada_w[:, h, :, :], a["w2_ada"][l, f * ADA_CHUNKS, h]).then_inc(ada_in[h], 16)
                with pool.Fori(1, ADA_CHUNKS) as c:
                    for h in range(2):
                        pool.wait_ge(ada_half[h], c + f * ADA_CHUNKS)
                        pool.dma_start(ada_w[:, h, :, :],
                                       a["w2_ada"][l, c + f * ADA_CHUNKS, h]).then_inc(ada_in[h], 16)

            for blk in (1, 2):
                with pool.Fori(0, LAYERS) as l:
                    width = P1_END if blk == 1 else P2_END
                    pool.dma_start(par[:, 0:width], a[f"params{blk}"][l]).then_inc(params_in, 16)
                    if blk == 1:
                        ada_loads(l, 0)
                        pool.wait_ge(scale_ready, 2 * NT + 1)
                        ada_loads(l, 1)
                    pool.wait_ge(layer_done, l * 3 + (3 + 3 * LAYERS * (blk - 1)))
                    pool.sem_inc(layers_closed, 1)
                    pool.sem_clear(cleared)
                    pool.sem_inc(layer_open, 1)

        def params_of(l, blk):
            return l * 16 + (16 if blk == 1 else 16 + 16 * LAYERS)

        def close_layer(eng, l, blk):
            eng.drain().then_inc(layer_done, 1)
            eng.wait_ge(layer_open, l + (1 + LAYERS * (blk - 1)))

        def turn_list(blk, order):
            return [[(i, source(blk, i), 64 if (blk, i) == (1, 6) else P) for i in pair] for pair in order]

        def source(blk, i):
            if blk == 1:
                if i < 2:
                    return lambda t: tok1[:, t, 3, P + i * P:P + (i + 1) * P]
                if i < 4:
                    return lambda t: dup1[:, t, i - 2, :]
                c = (i - 4) * P
                return lambda t: tok1[:, t, 2, c:min(c + P, DSA * HD)]
            if 4 <= i < 6:
                return lambda t: dup2[:, t, i - 4, :]
            c = i * P if i < 4 else 768 + (i - 6) * P
            return lambda t: tok2[:, t, c:c + P]

        TURNS = {1: turn_list(1, [(0, 1), (2, 3), (4, 5), (6,)]),
                 2: turn_list(2, [(0, 1), (4, 5), (2, 3), (6, 7), (10, 11), (8, 9), (12, 13)])}
        TURNED = {1: lambda i: (tt1[:, i, :], SCALE if i >= 4 else 1.0),
                  2: lambda i: (tt2[:, i, :], SCALE if i < 4 or 6 <= i < 10 else 1.0)}
        TOKENS = {1: {("ckv", 0): 1, ("turn", 0): 3, ("turn", 1): 5, ("turn", 2): 5, ("turn", 3): 5,
                      **{("fox", h): 2 for h in range(FOX)}},
                  2: {("turn", h): 1 if h < 3 else 2 for h in range(7)}}
        PREP = ("ckv", "kv", "turn", "idx")
        G_AT = {1: Walk(SLOTS1, FF1 + 8, 8, KD, Walk(SLOTS1, FF1 + 4, 4, KD, 8).groups_after).groups_after,
                2: Walk(SLOTS2, 6, 6, KD, 12).groups_after}
        @block.tensor
        def _(pe):
            state = {}

            def mm3(out, l_hi, l_lo, r_hi, r_lo, start, stop):
                pe.matmul(out, l_hi, r_hi, start=start, stop=False, skip_group_check=True)
                pe.matmul(out, l_hi, r_lo, start=False, stop=False, skip_group_check=True)
                return pe.matmul(out, l_lo, r_hi, start=False, stop=stop, skip_group_check=True)

            def wait_part(l, blk, kind, n):
                slots = SL[blk]
                count = n if not isinstance(n, int) else parts_before(slots, kind, n + 1) - 1
                pe.wait_ge(lo_ready[kind], l * parts_before(slots, kind, len(slots))
                           + lo_before(blk, kind) + count + 3)

            def wait_ffn_part(l, blk, kind, n0, j):
                slots = SL[blk]
                pe.wait_ge(lo_ready[kind], l * parts_before(slots, kind, len(slots))
                           + lo_before(blk, kind) + parts_before(slots, kind, n0) + j + 3)

            def norm(ada_before=False):
                n = state["norms"] = state.get("norms", 0) + 1
                for b in range(4):
                    if b == 3 and ada_before:
                        pe.wait_ge(ada_copied, 1)
                    for k in (2 * b, 2 * b + 1):
                        for t in range(NT):
                            if k == 0:
                                pe.wait_ge(scale_ready, NT * (n - 1) + t + 1)
                            m = pe.matmul(ps[:, b, (k % 2) * SEQ + t * P:(k % 2) * SEQ + (t + 1) * P],
                                          x[:, t, k * P:(k + 1) * P], scaled_id[:, t, :], start=True, stop=True,
                                          skip_group_check=True)
                    m.then_inc(turned, 1)
                state["h_waited"] = 0

            def need_h(k):
                if state["h_waited"] < k // 2 + 1:
                    state["h_waited"] = k // 2 + 1
                    pe.wait_ge(hlo_ready, 4 * (state["norms"] - 1) + k // 2 + 1)

            def feed_forward(l, blk, n0, tiles, gates, extra={}):
                state.setdefault("gated", 0)
                g0 = state["gated"]

                def gate_up(j, p):
                    wait_ffn_part(l, blk, 0, n0, j)
                    for m in range(gates):
                        for k in range(KD):
                            if isinstance(j, int) and j == 0:
                                need_h(k)
                            c = (m * KD + k) * P
                            last_mm = mm3(ps[:, p, m * SEQ:(m + 1) * SEQ], whi[0][:, p, c:c + P], wlo[0][:, p, c:c + P],
                                          hhi[:, k, :], hlo[:, k, :], k == 0, k == KD - 1)
                    last_mm.then_inc(used[0], 1)

                def down(j, p, first_tile, last_tile):
                    wait_ffn_part(l, blk, 1, n0, j)
                    pe.wait_ge(gated_ready, g0 + j + 1)
                    for t in range(NT):
                        for h in range(2):
                            last_mm = mm3(ps[:, 4 + 2 * t + h, :], ghi[:, p, t * P:(t + 1) * P],
                                          glo[:, p, t * P:(t + 1) * P],
                                          whi[1][:, p, h * 512:(h + 1) * 512], wlo[1][:, p, h * 512:(h + 1) * 512],
                                          first_tile, last_tile)
                            if last_tile and (t, h) != (NT - 1, 1):
                                last_mm.then_inc(sums_ready, 1)
                    last_mm.then_inc(used[1], 1)

                def step(j, p, turn):
                    gate_up(j, p)
                    if not (isinstance(j, int) and j == 0):
                        down(j - 1, 1 - p, isinstance(j, int) and j == 1, False)
                    if turn is None and j in extra:
                        extra[j]()

                feed_forward_steps(pe, tiles, step)
                down(tiles - 1, (tiles - 1) % 2, False, True)
                if blk == 1:
                    pe.wait_ge(ada_lo_ready, 1 if n0 == 0 else 2)
                    for i in range(ADA_CHUNKS * ADA // P):
                        c = slice(i * P, (i + 1) * P)
                        pe.matmul(ps[:, 3, 2 * i:2 * i + 2], ada_hi[:, c], ones_r[:, :], start=True, stop=False,
                                  skip_group_check=True)
                        m = pe.matmul(ps[:, 3, 2 * i:2 * i + 2], ada_lo[:, c], ones_r[:, :], start=False, stop=True,
                                      skip_group_check=True)
                    m.then_inc(ada_used, 1)
                state["gated"] += tiles

            def enter(l, blk, tile):
                n, kind, i, end = tile
                if i == 0:
                    wait_part(l, blk, kind, n)

            def finish(m, mark_is_group, tile):
                if tile[3]:
                    m.then_inc(used[tile[1]], 1)
                elif mark_is_group:
                    m.then_inc(group_done, 1)

            def weight(tile):
                n, kind, i, _ = tile
                return whi[kind][:, n % 2, i * P:(i + 1) * P], wlo[kind][:, n % 2, i * P:(i + 1) * P]

            def gate_tile(l, blk, walk, g):
                if g >= 2:
                    pe.wait_ge(gate_copied, g - 1)
                for k in range(KD):
                    tile = walk.tiles[g * KD + k]
                    enter(l, blk, tile)
                    hi, lo = weight(tile)
                    m = mm3(ps[:, g % 2, 0:SEQ], hi, lo, hhi[:, k, :], hlo[:, k, :], k == 0, k == KD - 1)
                    finish(m, k == KD - 1, tile)

            def project_turned(l, blk, walk, count, copied_before):
                for g in range(count):
                    pe.wait_ge(proj_copied, g + copied_before - 3)
                    for k in range(KD):
                        n, kind, _, _ = walk.tiles[g * KD + k]
                        need_h(k)
                        cols = (2, 1)[kind]
                        m_in = (g % 3) if kind == 0 else 0
                        if k == 0 and m_in == 0:
                            wait_part(l, blk, kind, n)
                        c = (k * cols + m_in) * P
                        m = mm3(ps[:, g % 4, 0:SEQ], whi[kind][:, n % 2, c:c + P], wlo[kind][:, n % 2, c:c + P],
                                hhi[:, k, :], hlo[:, k, :], k == 0, k == KD - 1)
                    if kind == 1 or m_in == 1:
                        m.then_inc(used[kind], 1)
                    else:
                        m.then_inc(group_done, 1)

            def project_rows(l, blk, n0, count, copied_before):
                g = copied_before
                for n in range(n0, n0 + count):
                    for kind in (0, 1):
                        wait_part(l, blk, kind, n)
                        w = (256, 128)[kind]
                        for t in range(NT):
                            if g >= 4:
                                pe.wait_ge(proj_copied, g - 3)
                            for k in range(KD):
                                need_h(k)
                                m = mm3(ps[:, g % 4, 0:w], hhi[:, k, t * P:(t + 1) * P], hlo[:, k, t * P:(t + 1) * P],
                                        whi[kind][:, n % 2, k * w:(k + 1) * w], wlo[kind][:, n % 2, k * w:(k + 1) * w],
                                        k == 0, k == KD - 1)
                            if t == NT - 1:
                                m.then_inc(used[kind], 1)
                            else:
                                m.then_inc(group_done, 1)
                            g += 1

            def bank_free(items, tick):
                back = tick - 2
                while back >= 0 and items[back] is None:
                    back -= 2
                if back >= 0:
                    kind = READ_BY[items[back][0]]
                    s = scores_taken if kind == "scores_taken" else prep_copied
                    pe.wait_ge(s, count_upto(items, back, lambda k: READ_BY[k] == kind))

            def scores(bank, qt, kt_, pb, forget):
                q, k_ = qt[pb:pb + HD, :], kt_[pb:pb + HD, :]
                pe.matmul(ps[:, bank, 0:P], q[:, 0:P], k_[:, 0:P], start=True, stop=forget is None, skip_group_check=True)
                if forget is not None:
                    pe.matmul(ps[:, bank, 0:P], fcast[:, forget, 0, :], consts[:, C_U:C_U + P],
                              start=False, stop=True, skip_group_check=True)
                m = pe.matmul(ps[:, bank, P:3 * P], q[:, P:SEQ], k_[:, 0:SEQ], start=True, stop=forget is None,
                              skip_group_check=True)
                if forget is not None:
                    pe.matmul(ps[:, bank, P:3 * P], fcast[:, forget, 0, :], consts[:, C_U:C_U + SEQ],
                              start=False, stop=False, skip_group_check=True)
                    m = pe.matmul(ps[:, bank, 2 * P:3 * P], fcast[:, forget, 1, :], consts[:, C_U:C_U + P],
                                  start=False, stop=True, skip_group_check=True)
                return m

            def item_scores(blk, items, tick):
                kind, h = items[tick]
                bank = 2 + tick % 2
                bank_free(items, tick)
                need = TOKENS[blk].get(items[tick])
                if need:
                    pe.wait_ge(tokens_ready, need)
                if kind in ("kv", "idx", "dsa", "swa", "moba"):
                    before = max(i for i in range(tick) if items[i] and items[i][0] in ("ckv", "kv", "turn"))
                    pe.wait_ge(prep_copied, count_upto(items, before, lambda k: k in PREP))
                m = None
                if kind == "fox":
                    m = scores(bank, qk1[:, 0, h // 2, :], qk1[:, 1, h // 2, :], HD * (h % 2), h)
                elif kind == "sb":
                    m = scores(bank, qk1[:, 2, h // 2, :], qk1[:, 3, h // 2, :], HD * (h % 2), None)
                elif kind == "idx":
                    m = scores(bank, tt1[:, h // 2, :], tt1[:, 2, :], HD * (h % 2), None)
                elif kind == "dsa":
                    m = scores(bank, tt1[:, 4 + h // 2, :], tt1[:, 3, :], HD * (h % 2), None)
                elif kind == "swa":
                    m = scores(bank, tt2[:, h // 2, :], tt2[:, 4 + h // 4, :], HD * (h % 2), None)
                elif kind == "moba":
                    m = scores(bank, tt2[:, 6 + h // 2, :], tt2[:, 10 + h // 2, :], HD * (h % 2), None)
                if kind in HEADS or kind == "idx":
                    if kind == "idx":
                        m.then_inc(prep_ready, 1)
                    else:
                        m.then_inc(scores_ready, 1)
                    return
                if kind == "ckv":
                    for t in range(NT):
                        m = pe.transpose(ps[:, bank, t * P:(t + 1) * P], tok1[:, t, 3, 0:P], ident)
                elif kind == "kv":
                    for t in range(NT):
                        m = pe.matmul(ps[:, bank, t * P:(t + 1) * P], kvt[:, t * P:(t + 1) * P],
                                      par[:, P1_WKV:P1_WKV + P], start=True, stop=True, skip_group_check=True)
                elif kind == "turn":
                    for i, src, w in TURNS[blk][h]:
                        for t in range(NT):
                            m = pe.transpose(ps[0:w, bank, (i % 2) * SEQ + t * P:(i % 2) * SEQ + (t + 1) * P],
                                             src(t), ident)
                m.then_inc(prep_ready, 1)

            def item_turn(blk, items, tick):
                if tick < 0 or tick >= len(items) or not items[tick] or items[tick][0] not in HEADS:
                    return
                e = count_upto(items, tick, lambda k: k in HEADS)
                pe.wait_ge(probs_ready, e)
                if e > 2:
                    pe.wait_ge(pt_copied, e - 2)
                s = (sm if blk == 1 else sm2)
                for b in range(3):
                    m = pe.transpose(ps[:, 4 + e % 2, b * P:(b + 1) * P], s[:, tick % 3, b * P:(b + 1) * P], ident)
                m.then_inc(pt_ready, 1)

            def item_values(blk, items, tick):
                if tick < 0 or tick >= len(items) or not items[tick] or items[tick][0] not in HEADS:
                    return
                kind, h = items[tick]
                e = count_upto(items, tick, lambda k: k in HEADS)
                pe.wait_ge(pt_copied, e)
                if e > 2:
                    pe.wait_ge(y_done, e - 2)
                q = (pts if blk == 1 else pts2)[:, e % 2, :]
                bank = 6 + e % 2

                def v(t):
                    if kind == "fox":
                        return tok1[:, t, 0, h * HD:(h + 1) * HD]
                    if kind == "sb":
                        return tok1[:, t, 1, h * HD:(h + 1) * HD]
                    if kind == "dsa":
                        return kvv[:, t, HD:2 * HD]
                    if kind == "swa":
                        return tok2[:, t, 640 + (h // 4) * HD:640 + (h // 4 + 1) * HD]
                    return tok2[:, t, 1792 + h * HD:1792 + (h + 1) * HD]

                pe.matmul(ps[:, bank, 0:HD], q[:, 0:P], v(0), start=True, stop=True, skip_group_check=True)
                pe.matmul(ps[:, bank, HD:2 * HD], q[:, P:2 * P], v(0), start=True, stop=False, skip_group_check=True)
                pe.matmul(ps[:, bank, HD:2 * HD], q[:, 2 * P:3 * P], v(1), start=False, stop=True,
                          skip_group_check=True).then_inc(pv_ready, 1)

            def ticks(l, blk, items, gates, walk):
                pe.wait_ge(proj_copied, 28 if blk == 1 else 24)
                if blk == 2:
                    pe.wait_ge(gain_copied, 2)
                for tick in range(max(len(items) + 3, gates)):
                    if tick < gates:
                        gate_tile(l, blk, walk, tick)
                    if tick < len(items) and items[tick]:
                        item_scores(blk, items, tick)
                    item_turn(blk, items, tick - 2)
                    item_values(blk, items, tick - 3)

            def turn_y(blk, tiles, heads):
                pe.wait_ge(y_done, heads)
                pe.wait_ge(gate_copied, 24 if blk == 1 else 16)
                y = y1 if blk == 1 else y2
                for i in range(tiles):
                    b = (i // 2) % 4
                    if i % 2 == 0 and i // 2 >= 4:
                        pe.wait_ge(ylo_ready, i // 2 - 3)
                    for t in range(NT):
                        m = pe.transpose(ps[:, b, (i % 2) * SEQ + t * P:(i % 2) * SEQ + (t + 1) * P],
                                         y[:, t, i * P:(i + 1) * P], ident)
                    if i % 2 == 1 or i == tiles - 1:
                        m.then_inc(y_turned, 1)

            def up_and_out(l, blk, up_walk, tiles, branches, out_n0):
                pe.wait_ge(ylo_ready, (tiles + 1) // 2)
                for f in range(KD):
                    if f >= 4:
                        pe.wait_ge(merged_ready, f - 3)
                    per = tiles // branches
                    for i in range(tiles):
                        tile = up_walk.tiles[f * tiles + i]
                        enter(l, blk, tile)
                        hi, lo = weight(tile)
                        br = i // per
                        bank = UP_BANKS[f % 4] + br // 2
                        m = mm3(ps[:, bank, (br % 2) * SEQ:(br % 2 + 1) * SEQ], hi, lo, yhi[:, i, :], ylo[:, i, :],
                                i % per == 0, i % per == per - 1)
                        finish(m, i == tiles - 1, tile)
                pe.wait_ge(merged_ready, KD - 2)
                kt_ = 0
                for n in range(out_n0, out_n0 + 3):
                    for kind in (0, 1):
                        rows = SL[blk][n][kind] // KD
                        if rows:
                            wait_part(l, blk, kind, n)
                        if not rows:
                            continue
                        last_part = kt_ + rows == KD
                        if last_part:
                            pe.wait_ge(merged_ready, KD)
                        order = [(r, t, h) for r in range(rows) for t in range(NT) for h in range(2)]
                        if last_part:
                            order = [(r, t, h) for t in range(NT) for h in range(2) for r in range(rows)]
                        for r, t, h in order:
                            k = kt_ + r
                            c = r * D + h * 512
                            m = mm3(ps[:, 4 + 2 * t + h, :], hhi[:, k, t * P:(t + 1) * P],
                                    hlo[:, k, t * P:(t + 1) * P], whi[kind][:, n % 2, c:c + 512],
                                    wlo[kind][:, n % 2, c:c + 512], k == 0, k == KD - 1)
                            if last_part and r == rows - 1 and (t, h) != (NT - 1, 1):
                                m.then_inc(sums_ready, 1)
                        kt_ += rows
                        m.then_inc(used[kind], 1)

            def spread_gain(bank, count):
                pe.wait_ge(diag_ready, count)
                pe.matmul(ps[:, bank, :], ones, diag[:, :, :].rearrange("p a b -> p (a b)"),
                          start=True, stop=True, skip_group_check=True).then_inc(spread, 1)

            pe.wait_ge(consts_in, 16)
            pe.wait_ge(x_in, 16)
            for blk in (1, 2):
                with pe.Fori(0, LAYERS) as l:
                    state.clear()
                    if blk == 1:
                        norm()
                        feed_forward(l, 1, 0, FF1, 2)
                        norm(ada_before=True)
                        project_rows(l, 1, FF1, 4, 0)
                        project_turned(l, 1, Walk(SLOTS1, FF1 + 4, 4, KD, 8), 12, 16)
                        pe.wait_ge(params_in, params_of(l, blk))
                        ticks(l, 1, schedule1(), 24, Walk(SLOTS1, FF1 + 8, 8, KD, 0))
                        turn_y(1, YT1, FOX + SB + DSA)
                        up_and_out(l, 1, Walk(SLOTS1, FF1 + 16, 3, YT1, 0), YT1, 3, FF1 + 19)
                        norm()
                        feed_forward(l, 1, FF1 + 22, FF1, 2)
                    else:
                        norm()
                        project_rows(l, 2, 0, 5, 0)
                        spread_gain(4, 1)
                        project_rows(l, 2, 5, 1, 20)
                        spread_gain(5, 2)
                        ticks(l, 2, schedule2(), 16, Walk(SLOTS2, 6, 6, KD, 0))
                        turn_y(2, YT2, SWA + MOBA)
                        up_and_out(l, 2, Walk(SLOTS2, 12, 3, YT2, 0), YT2, 2, 15)
                        norm()
                        feed_forward(l, 2, 18, FF2, 1, {1: lambda: spread_gain(2, 3), 2: lambda: spread_gain(3, 4)})
                    close_layer(pe, l, blk)

        @block.scalar
        def _(act):
            chain = Count(act, act_chain)
            state = {}

            def seen(s, name, k=1):
                state[name] = state.get(name, 0) + k
                act.wait_ge(s, state[name])

            def split_high(l, blk, kind, n, p=None, j=None, n0=None):
                slots = SL[blk]
                if j is None:
                    if n >= len(slots) or not slots[n][kind]:
                        return
                    p, width = n % 2, slots[n][kind] * P
                    seq = sum(1 for i in range(n) if i % 2 == p and slots[i][kind])
                    reuse = parts_before(slots, kind, n - 1) if n >= 2 else 0
                else:
                    width = slots[n0][kind] * P
                    seq = sum(1 for i in range(n0) if i % 2 == 0 and slots[i][kind]) if p == 0 else \
                        sum(1 for i in range(n0) if i % 2 == 1 and slots[i][kind])
                    seq = seq + j[1]
                    reuse = parts_before(slots, kind, n0) + j[0] - 1
                act.wait_ge(land[kind][p], l * (16 * per_layer(blk, kind, p)) + seq * 16
                            + (16 * landed_before(blk, kind, p) + 16))
                if not isinstance(reuse, int) or reuse > 0:
                    act.wait_ge(used[kind], reuse)
                act.activation(whi[kind][:, p, 0:width], raw[kind][:, p, 0:width], ACT.Copy).then_inc(hi_ready[kind], 1)

            def norm(cols, shifts=None, between=None, after=None):
                def square(t, h):
                    seen(x_ready, "x")
                    c = slice(h * 512, (h + 1) * 512)
                    return act.activation(xn[:, t, c], x[:, t, c], ACT.Square, accum_out=ms[:, 2 * t + h:2 * t + h + 1])

                for t in range(NT):
                    chain(square(t, 0))
                    chain.also(act.activation(half_ms[:, t:t + 1], ms[:, 2 * t:2 * t + 1], ACT.Identity,
                                              scale=1.0 / D, bias=eps))
                    square(t, 1).then_inc(squares_ready, 1)
                    seen(squares_ready, "squares")
                    act.wait_ge(act_chain, chain.value())
                    chain(act.activation(rs0[:, t:t + 1], ms[:, 2 * t + 1:2 * t + 2], ACT.Ln, scale=1.0 / D,
                                         bias=half_ms[:, t:t + 1]))
                act.activation(rs0[:, 0:NT], rs0[:, 0:NT], ACT.Exp, scale=-0.5).then_inc(guess_ready, 1)
                if between:
                    between()
                for b in range(4):
                    seen(turned, "turned")
                    for k in (2 * b, 2 * b + 1):
                        m = act.activation(hhi[:, k, :], ps[:, b, (k % 2) * SEQ:(k % 2 + 1) * SEQ], ACT.Identity,
                                           scale=cols(k), bias=0.0 if shifts is None else shifts(k))
                        if k % 2 == 0:
                            chain.also(m)
                    m.then_inc(hhi_ready, 1)
                if after:
                    after()

            def rsqrt(width, scale):
                chain(act.activation(rs0[:, 0:width], ms[:, 0:width], ACT.Ln, scale=scale, bias=eps))
                act.activation(rs0[:, 0:width], rs0[:, 0:width], ACT.Exp, scale=-0.5).then_inc(guess_ready, 1)

            eps = small[:, 60:61]

            def feed_forward(l, blk, n0, tiles, gates, extra={}):
                def step(j, p, i):
                    act.wait_ge(used[0], j + (n0 + 1))
                    if gates == 2:
                        act.activation(ex[:, p, :], ps[:, p, 0:SEQ], ACT.Tanh, scale=0.5).then_inc(act_ready, 1)
                    else:
                        act.activation(ex[:, p, :], ps[:, p, 0:SEQ], ACT.Relu).then_inc(act_ready, 1)
                    if isinstance(j, int):
                        split_high(l, blk, 0, n0 + j + 2)
                        split_high(l, blk, 1, n0 + j + 1)
                    else:
                        u = 0 if p == 1 else 1
                        split_high(l, blk, 0, None, p, (j + 2, i + (2 if u == 0 else 3)), n0)
                        split_high(l, blk, 1, None, 1 - p, (j + 1, i + 2), n0)
                    if i is None and j in extra:
                        extra[j]()
                    if blk == 1 and i is None and j == tiles - 3:
                        f = 0 if n0 == 0 else 1
                        act.wait_ge(ada_half[1], (f + 1) * ADA_CHUNKS)
                        act.activation(ada_hi[:, :], ada_acc[:, :], ACT.Copy).then_inc(ada_hi_ready, 1)

                if gates == 2:
                    act.preload_act_table_set("exp_and_others")

                feed_forward_steps(act, tiles, step)
                if gates == 2:
                    act.preload_act_table_set("natural_log_exp_and_others")

            def copy_projection(mark, out, src, scale):
                sem_, val = mark
                act.wait_ge({"a": used[0], "b": used[1], "g": group_done}[sem_], val)
                act.activation(out, src, ACT.Copy, scale=scale).then_inc(proj_copied, 1)

            def project_turned(l, blk, n0, groups_before):
                w = Walk(SL[blk], n0, 4, KD, groups_before)
                for g in range(12):
                    s, m = g // 3, g % 3
                    if m == 0:
                        split_high(l, blk, 1, n0 + s + 1)
                        if s == 1:
                            token_rsqrt(4)
                            token_exp_log()
                    copy_projection(w.mark[g], qk1[:, s, m, :], ps[:, g % 4, 0:SEQ], SCALE if s in (0, 2) else 1.0)
                    if m == 1:
                        split_high(l, blk, 0, n0 + s + 2)
                return w.groups_after

            def project_rows(l, blk, n0, count, g, done_groups):
                for n in range(n0, n0 + count):
                    split_high(l, blk, 1, n + 1)
                    if blk == 2 and n == 3:
                        token_rsqrt(20)
                    for kind in (0, 1):
                        for t in range(NT):
                            if t == NT - 1:
                                mark = ("ab"[kind], parts_before(SL[blk], kind, n + 1))
                            else:
                                done_groups += 1
                                mark = ("g", done_groups)
                            w = (256, 128)[kind]
                            if blk == 1:
                                out = tok1[:, t, 3 - (n - n0), kind * 256:kind * 256 + w]
                            else:
                                c = n * 384 + kind * 256
                                out = tok2[:, t, c:c + w]
                            copy_projection(mark, out, ps[:, g % 4, 0:w], 1.0)
                            g += 1
                        if kind == 0:
                            split_high(l, blk, 0, n + 2)
                return done_groups

            def item_softmax(blk, items, tick):
                kind, h = items[tick]
                s = (sm if blk == 1 else sm2)[:, tick % 3, :]
                bank = 2 + tick % 2
                if kind in ("fox", "dsa", "swa", "moba"):
                    e = count_upto(items, tick, lambda k: k in ("fox", "dsa", "swa", "moba"))
                    act.wait_ge(max_ready, e)
                    if kind == "swa":
                        chain.also(act.activation(sinkexp[:, tick, :], rowmax[:, tick, :], ACT.Exp,
                                                  bias=par[:, P2_SINK + h:P2_SINK + h + 1]))
                    chain.also(act.activation(s[:, 0:P], s[:, 0:P], ACT.Exp, bias=rowmax[:, tick, 0:1],
                                              accum_out=rowsum[:, tick, 0:1]))
                    act.activation(s[:, P:3 * P], s[:, P:3 * P], ACT.Exp, bias=rowmax[:, tick, 1:2],
                                   accum_out=rowsum[:, tick, 1:2]).then_inc(probs_ready, 1)

            def stick_exp(items, tick):
                if 0 <= tick < len(items) and items[tick] and items[tick][0] == "sb":
                    act.wait_ge(stick_ready, count_upto(items, tick, lambda k: k == "sb"))
                    s = sm[:, tick % 3, :]
                    act.activation(s, s, ACT.Exp).then_inc(probs_ready, 1)

            def item_early(blk, items, tick):
                kind, h = items[tick]
                bank = 2 + tick % 2
                if kind == "sb":
                    e = count_upto(items, tick, lambda k: k == "sb")
                    act.wait_ge(abs_ready, e)
                    chain(act.activation(aux[:, tick % 2, :], aux[:, tick % 2, :], ACT.Exp, scale=-1.0))
                    act.activation(aux[:, tick % 2, :], aux[:, tick % 2, :], ACT.Ln, bias=1.0).then_inc(log_ready, 1)
                elif kind in ("ckv", "kv", "turn", "idx"):
                    e = count_upto(items, tick, lambda k: k in ("ckv", "kv", "turn", "idx"))
                    act.wait_ge(prep_ready, e)
                    if kind == "ckv":
                        act.activation(kvt[:, :], ps[:, bank, 0:SEQ], ACT.Identity,
                                       scale=par[:, P1_GKV:P1_GKV + 1]).then_inc(prep_copied, 1)
                    elif kind == "kv":
                        act.activation(kvv[:, :, :].rearrange("p t c -> p (t c)"), ps[:, bank, 0:SEQ],
                                       ACT.Copy).then_inc(prep_copied, 1)
                    elif kind == "idx":
                        if h >= 3:
                            act.wait_ge(index_added, h - 2)
                        act.activation(sm[:, tick % 3, :], ps[:, bank, 0:384], ACT.Relu).then_inc(prep_copied, 1)
                    else:
                        todo = TURNS[blk][h]
                        for q, (i, _, w) in enumerate(todo):
                            dst, scale = TURNED[blk](i)
                            m = act.activation(dst[0:w, :], ps[0:w, bank, (i % 2) * SEQ:(i % 2 + 1) * SEQ], ACT.Copy,
                                               scale=scale)
                            if q < len(todo) - 1:
                                chain.also(m)
                        m.then_inc(prep_copied, 1)

            def item_copy(blk, items, tick):
                if tick < 0 or tick >= len(items) or not items[tick] or items[tick][0] not in HEADS:
                    return
                e = count_upto(items, tick, lambda k: k in HEADS)
                act.wait_ge(pt_ready, e)
                act.activation((pts if blk == 1 else pts2)[:, e % 2, :], ps[:, 4 + e % 2, 0:384],
                               ACT.Copy).then_inc(pt_copied, 1)

            def gate_tile(blk, walk, tick, gates):
                mark = walk.mark[tick]
                act.wait_ge({"a": used[0], "b": used[1], "g": group_done}[mark[0]], mark[1])
                act.activation((g1 if blk == 1 else g2)[:, tick, :], ps[:, tick % 2, 0:SEQ],
                               ACT.Copy).then_inc(gate_copied, 1)

            def gate_tanh(blk, f):
                n = BRANCH1 if blk == 1 else BRANCH2
                g = (g1 if blk == 1 else g2)[:, f * n:(f + 1) * n, :].rearrange("p a b -> p (a b)")
                act.wait_ge(gate_copied, (f + 1) * n)
                act.activation(g, g, ACT.Tanh, scale=0.5).then_inc(gates_ready, 1)

            def ticks(l, blk, items, gates, walk, n0):
                first_tanh = len(items) + 3 - KD
                assert all(i is None or i[0] != "sb" for i in items[first_tanh:])
                for tick in range(max(len(items) + 3, gates)):
                    item_copy(blk, items, tick - 3)
                    stick_exp(items, tick - 1)
                    if tick < gates and tick % 3 == 0:
                        split_high(l, blk, 1, n0 + tick // 3 + 1)
                    if tick in TOKEN_WORK_ACT[blk]:
                        TOKEN_WORK_ACT[blk][tick]()
                    if tick < gates:
                        gate_tile(blk, walk, tick, gates)
                        if tick % 3 == 1 or (blk == 2 and tick == 15):
                            split_high(l, blk, 0, n0 + tick // 3 + 2)
                    if tick < len(items) and items[tick]:
                        item_early(blk, items, tick)
                        item_softmax(blk, items, tick)
                    if tick == first_tanh - 1:
                        act.preload_act_table_set("exp_and_others")
                    if first_tanh <= tick < first_tanh + KD:
                        gate_tanh(blk, tick - first_tanh)
                act.preload_act_table_set("natural_log_exp_and_others")
                return walk.groups_after

            def token_exp_log():
                act.wait_ge(tok_ask, 1)
                chain(act.activation(fsp[:, 1, :, :], fsp[:, 1, :, :], ACT.Exp, scale=-1.0))
                act.activation(fsp[:, 1, :, :], fsp[:, 1, :, :], ACT.Ln, bias=1.0).then_inc(tok_answer, 1)

            def token_rsqrt(width):
                seen(ms_ready, "ms")
                rsqrt(width, 1.0)

            TOKEN_WORK_ACT = {1: {},
                              2: {0: lambda: token_rsqrt(32)}}

            def turn_y(blk, tiles):
                for i in range(0, tiles, 2):
                    w = min(2, tiles - i)
                    seen(y_turned, "y_turned")
                    act.activation(yhi[:, i:i + w, :].rearrange("p a b -> p (a b)"), ps[:, (i // 2) % 4, 0:w * SEQ],
                                   ACT.Copy, scale=0.5).then_inc(yhi_ready, 1)

            def up_and_out(l, blk, n0):
                for n in range(n0, n0 + 6):
                    split_high(l, blk, 1, n + 1)
                    if n < n0 + 5:
                        split_high(l, blk, 0, n + 2)

            def gain_row(bank, h):
                seen(spread, "spread")
                act.activation(gtb[:, h * 512:(h + 1) * 512], ps[:, bank, :], ACT.Copy).then_inc(gain_copied, 1)

            act.preload_act_table_set("natural_log_exp_and_others")
            act.wait_ge(small_in, 32)
            act.wait_ge(setup_chain, 1)
            act.activation(small[:, 16:24], csilu[:, :], ACT.Exp, scale=-1.0).then_inc(setup_chain, 1)
            act.wait_ge(x_in, 16)
            for blk in (1, 2):
                if blk == 2:
                    for t in range(NT):
                        act.activation(xn[:, t, :], x[:, t, :], ACT.Square, accum_out=ms[:, t:t + 1]).then_inc(between, 1)
                    act.wait_ge(between, 2)
                    act.activation(rs0[:, 0:NT], ms[:, 0:NT], ACT.Ln, scale=1.0 / D, bias=eps).then_inc(between, 1)
                    act.wait_ge(between, 3)
                    act.activation(rs0[:, 0:NT], rs0[:, 0:NT], ACT.Exp, scale=-0.5).then_inc(between, 1)
                    act.wait_ge(angles_ready, 1)
                    act.activation(rope2[:, :, :, :], rope2[:, :, :, :], ACT.Sin).then_inc(tables_ready, 1)
                    act.preload_act_table_set("natural_log_exp_and_others")
                    act.wait_ge(between, 10)
                with act.Fori(0, LAYERS) as l:
                    state.clear()
                    chain.n = 0
                    starts = dict(between=lambda: split_high(l, blk, 0, 0),
                                  after=lambda: (split_high(l, blk, 1, 0), split_high(l, blk, 0, 1)))
                    if blk == 1:
                        act.wait_ge(params_in, params_of(l, blk))
                        norm(lambda k: par[:, P1_G + k:P1_G + k + 1], **starts)
                        feed_forward(l, 1, 0, FF1, 2)
                        norm(lambda k: par[:, P1_G + 8 + k:P1_G + 9 + k])
                        done_groups = project_rows(l, 1, FF1, 4, 0, 0)
                        done_groups = project_turned(l, 1, FF1 + 4, done_groups)
                        w = Walk(SLOTS1, FF1 + 8, 8, KD, done_groups)
                        ticks(l, 1, schedule1(), 24, w, FF1 + 8)
                        turn_y(1, YT1)
                        up_and_out(l, 1, FF1 + 16)
                        norm(lambda k: par[:, P1_G + 16 + k:P1_G + 17 + k], after=lambda: split_high(l, 1, 0, FF1 + 23))
                        feed_forward(l, 1, FF1 + 22, FF1, 2)
                    else:
                        act.wait_ge(params_in, params_of(l, blk))
                        act.wait_ge(mod_ready, 1)
                        norm(lambda k: ncol[:, k:k + 1], lambda k: mod[:, k:k + 1], **starts)
                        done_groups = project_rows(l, 2, 0, 5, 0, 0)
                        gain_row(4, 0)
                        done_groups = project_rows(l, 2, 5, 1, 20, done_groups)
                        gain_row(5, 1)
                        w = Walk(SLOTS2, 6, 6, KD, done_groups)
                        ticks(l, 2, schedule2(), 16, w, 6)
                        turn_y(2, YT2)
                        up_and_out(l, 2, 12)
                        norm(lambda k: ncol[:, KD + k:KD + k + 1], lambda k: mod[:, 24 + k:25 + k],
                             after=lambda: split_high(l, 2, 0, 19))
                        feed_forward(l, 2, 18, FF2, 1, {1: lambda: gain_row(2, 0), 2: lambda: gain_row(3, 1)})
                    close_layer(act, l, blk)

        @block.vector
        def _(dve):
            chain = Count(dve, dve_chain)
            state = {}

            def seen(s, name, k=1):
                state[name] = state.get(name, 0) + k
                dve.wait_ge(s, state[name])

            def split_low(l, blk, kind, n, p=None, j=None, n0=None):
                slots = SL[blk]
                if j is None:
                    if n >= len(slots) or not slots[n][kind]:
                        return
                    p, width, count = n % 2, slots[n][kind] * P, parts_before(slots, kind, n + 1)
                else:
                    width, count = slots[n0][kind] * P, j + (parts_before(slots, kind, n0) + 1)
                dve.wait_ge(hi_ready[kind], count)
                dve.tensor_tensor(wlo[kind][:, p, 0:width], raw[kind][:, p, 0:width],
                                  whi[kind][:, p, 0:width].bitcast(F32), ALU.subtract).then_inc(lo_ready[kind], 1)

            def newton(width, scale):
                seen(guess_ready, "guess")
                w = slice(0, width)
                chain(dve.tensor_scalar(ms[:, w], ms[:, w], scale, EPS, ALU.mult, ALU.add))
                chain(dve.tensor_tensor(rt[:, w], rs0[:, w], ms[:, w], ALU.mult))
                chain(dve.scalar_tensor_tensor(rt[:, w], rt[:, w], -0.5, rs0[:, w], ALU.mult, ALU.mult))
                chain(dve.scalar_tensor_tensor(rstd[:, w], rt[:, w], 1.5, rs0[:, w], ALU.add, ALU.mult))

            def norm(cols, shifts=None, between=None, after=None):
                seen(squares_ready, "squares", NT)
                halves = ms[:, 0:2 * NT].rearrange("p (t h) -> p t h", h=2)[:, :, 1]
                chain(dve.scalar_tensor_tensor(ms[:, 8:8 + NT], halves, 1.0 / D, half_ms[:, :], ALU.mult, ALU.add))
                seen(guess_ready, "guess")
                chain(dve.tensor_tensor(rt[:, 0:NT], rs0[:, 0:NT], ms[:, 8:8 + NT], ALU.mult))
                chain(dve.scalar_tensor_tensor(rt[:, 0:NT], rt[:, 0:NT], -0.5, rs0[:, 0:NT], ALU.mult, ALU.mult))
                chain(dve.scalar_tensor_tensor(rstd[:, 0:NT], rt[:, 0:NT], 1.5, rs0[:, 0:NT], ALU.add, ALU.mult))
                for t in range(NT):
                    dve.tensor_scalar(scaled_id[:, t, :], ident, rstd[:, t:t + 1], None, ALU.mult).then_inc(scale_ready, 1)
                if between:
                    between()
                for b in range(4):
                    seen(hhi_ready, "hhi")
                    for k in (2 * b, 2 * b + 1):
                        src = ps[:, b, (k % 2) * SEQ:(k % 2 + 1) * SEQ]
                        high = hhi[:, k, :].bitcast(F32)
                        if shifts is None:
                            m = dve.scalar_tensor_tensor(hlo[:, k, :], src, cols(k), high, ALU.mult, ALU.subtract)
                        else:
                            tmp = (fd, fq)[k % 2]
                            chain(dve.tensor_scalar(tmp[:, :], src, cols(k), shifts(k), ALU.mult, ALU.add))
                            m = dve.tensor_tensor(hlo[:, k, :], tmp[:, :], high, ALU.subtract)
                        if k % 2 == 0:
                            chain.also(m)
                    m.then_inc(hlo_ready, 1)
                if after:
                    after()

            def feed_forward(l, blk, n0, tiles, gates, extra={}):
                e0 = state.get("ffn", 0)
                chain.per = 12 if gates == 2 else 4
                f = 0 if n0 == 0 else 1

                def step(j, p, turn):
                    gated = fa if gates == 2 or p == 0 else fq
                    if gates == 2:
                        c = f * ADA_CHUNKS + (0 if turn is None else turn + 1)
                        with_ada = turn is not None or j in (1, 2)
                        half = 1 - p
                        if with_ada:
                            dve.wait_ge(ada_in[half], l * (32 * ADA_CHUNKS) + c * 16 + 16)
                            if half:
                                dve.wait_ge(ada_half[0], c + 1)

                        def ada_part(k):
                            if not with_ada:
                                return
                            acc = ada_acc[:, 0:ADA] if turn is None else ada_acc[:, bass.ds((turn + 1) * ADA, ADA)]
                            w, cs = ada_w[:, half, k, :], csilu[:, half * 4 + k:half * 4 + k + 1]
                            if half == 0 and k == 0:
                                m = dve.tensor_scalar(acc, w, cs, None, ALU.mult)
                            else:
                                m = dve.scalar_tensor_tensor(acc, w, cs, acc, ALU.mult, ALU.add)
                            if k < 3:
                                chain.also(m)
                                if k:
                                    chain.behind()
                            else:
                                m.then_inc(ada_half[half], 1)

                        wait = chain.behind if with_ada else (lambda: dve.wait_ge(dve_chain, chain.value()))
                        ada_part(0)
                        dve.wait_ge(act_ready, j + (e0 + 1))
                        chain.also(dve.scalar_tensor_tensor(fq[:, :], ex[:, p, :], 1.0, ps[:, p, 0:SEQ], ALU.add, ALU.mult))
                        if with_ada:
                            chain.behind()
                        ada_part(1)
                        if not with_ada:
                            wait()
                        chain.also(dve.tensor_tensor(fa[:, :], ps[:, p, SEQ:2 * SEQ], fq[:, :], ALU.mult))
                        if with_ada:
                            chain.behind()
                        ada_part(2)
                        if not with_ada:
                            wait()
                        chain.also(dve.tensor_copy(ghi[:, p, :], gated[:, :]))
                        if with_ada:
                            chain.behind()
                        ada_part(3)
                        dve.wait_ge(dve_chain, chain.value())
                        dve.tensor_tensor(glo[:, p, :], gated[:, :], ghi[:, p, :].bitcast(F32),
                                          ALU.subtract).then_inc(gated_ready, 1)
                        if turn is None and j == tiles - 2:
                            dve.wait_ge(ada_hi_ready, f + 1)
                            dve.tensor_tensor(ada_lo[:, :], ada_acc[:, :], ada_hi[:, :].bitcast(F32),
                                              ALU.subtract).then_inc(ada_lo_ready, 1)
                    else:
                        dve.wait_ge(act_ready, j + (e0 + 1))
                        chain(dve.tensor_tensor(gated[:, :], ex[:, p, :], ex[:, p, :], ALU.mult))
                        chain(dve.tensor_copy(ghi[:, p, :], gated[:, :]))
                        dve.tensor_tensor(glo[:, p, :], gated[:, :], ghi[:, p, :].bitcast(F32),
                                          ALU.subtract).then_inc(gated_ready, 1)
                    if turn is None and n0 + j < FF1 - 1 or turn is None and n0:
                        split_low(l, blk, 0, n0 + j + 2)
                        split_low(l, blk, 1, n0 + j + 1)
                    elif turn is None:
                        pass
                    else:
                        split_low(l, blk, 0, None, p, j + 2, n0)
                        split_low(l, blk, 1, None, 1 - p, j + 1, n0)
                    if turn is None and j in extra:
                        extra[j]()

                feed_forward_steps(dve, tiles, step, chain)
                state["ffn"] = e0 + tiles
                for t in range(NT):
                    for h in range(2):
                        sum_complete(t, h, used[1], parts_before(SL[blk], 1, n0 + tiles))
                        c = slice(h * 512, (h + 1) * 512)
                        if blk == 1:
                            dve.scalar_tensor_tensor(x[:, t, c], ps[:, 4 + 2 * t + h, :], 0.25, x[:, t, c],
                                                     ALU.mult, ALU.add).then_inc(x_ready, 1)
                        else:
                            if t == 0 and h == 0:
                                seen(gain_copied, "gain", 2)
                            gained_residual(t, h)

            def keep_ada(l, f):
                dve.wait_ge(ada_used, f + 1)
                sums = ps[:, 3, 0:MOD].rearrange("p (c two) -> p c two", two=2)[:, :, 0]
                dve.tensor_copy(mod_raw[:, bass.ds(l * MOD + f * (MOD // 2), MOD // 2)], sums).then_inc(ada_copied, 1)

            def sum_complete(t, h, last_sem, last_value):
                if (t, h) == (NT - 1, 1):
                    dve.wait_ge(last_sem, last_value)
                else:
                    seen(sums_ready, "sums")

            def gained_residual(t, h):
                c = slice(h * 512, (h + 1) * 512)
                chain(dve.tensor_tensor(xn[:, t, c], ps[:, 4 + 2 * t + h, :], gtb[:, c], ALU.mult))
                dve.tensor_tensor(x[:, t, c], x[:, t, c], xn[:, t, c], ALU.add).then_inc(x_ready, 1)

            def gain_diagonals(g0, h):
                if h:
                    seen(spread, "spread", 2 if g0 != 16 else 1)
                cols = mod[:, g0 + 4 * h:g0 + 4 * h + 4]
                dve.tensor_tensor(diag[:, :, :], ident.unsqueeze(1).broadcast_to([P, 4, P]),
                                  cols.unsqueeze(2).broadcast_to([P, 4, P]), ALU.mult).then_inc(diag_ready, 1)

            def projections(l, blk, n0, count, work={}):
                for n in range(n0, n0 + count):
                    split_low(l, blk, 1, n + 1)
                    split_low(l, blk, 0, n + 2)
                    if n - n0 in work:
                        work[n - n0]()

            def item_early(blk, items, tick):
                kind, h = items[tick]
                s = (sm if blk == 1 else sm2)[:, tick % 3, :]
                bank = 2 + tick % 2
                if kind in HEADS:
                    e = count_upto(items, tick, lambda k: k in HEADS)
                    dve.wait_ge(scores_ready, e)
                    turned_before = heads_before(items, tick)
                    if turned_before:
                        dve.wait_ge(pt_ready, turned_before)
                    m = {"fox": mask(C_CAUSAL), "moba": mask(C_CAUSAL), "swa": mask(C_BAND), "sb": mask(C_STRICT),
                         "dsa": selmask[:, :]}[kind]
                    if kind == "sb":
                        dve.tensor_tensor(s, ps[:, bank, 0:384], m, ALU.add).then_inc(scores_taken, 1)
                        dve.wait_ge(scores_taken, e)
                        dve.scalar_tensor_tensor(aux[:, tick % 2, :], s, -1.0, s, ALU.mult, ALU.max).then_inc(abs_ready, 1)
                        return
                    chain.also(dve.tensor_tensor_reduce(s[:, 0:P], ps[:, bank, 0:P], m[:, 0:P], 1.0, PICKED,
                                                        ALU.add, ALU.max, rowmax[:, tick, 0:1]))
                    dve.tensor_tensor_reduce(s[:, P:3 * P], ps[:, bank, P:3 * P], m[:, P:3 * P], 1.0, PICKED,
                                             ALU.add, ALU.max, rowmax[:, tick, 1:2]).then_inc(scores_taken, 1)
                    dve.wait_ge(scores_taken, e)
                    dve.wait_ge(dve_chain, chain.value())
                    if kind == "swa":
                        m = dve.tensor_scalar(rowmax[:, tick, :], rowmax[:, tick, :], -1.0, small[:, 32 + h:33 + h],
                                              ALU.mult, ALU.min)
                    else:
                        m = dve.tensor_scalar(rowmax[:, tick, :], rowmax[:, tick, :], -1.0, None, ALU.mult)
                    m.then_inc(max_ready, 1)
                elif kind == "idx":
                    dve.wait_ge(prep_copied, count_upto(items, tick, lambda k: k in PREP))
                    for t, c in ((0, slice(0, P)), (1, slice(P, 3 * P))):
                        base = consts[:, C_CHUNK + c.start:C_CHUNK + c.stop] if h == 0 else iscore[:, c]
                        m = dve.scalar_tensor_tensor(iscore[:, c], s[:, c], tok1[:, t, 1, 320 + h:321 + h], base,
                                                     ALU.mult, ALU.add)
                        if t == 0:
                            chain.also(m)
                    m.then_inc(index_added, 1)
                    dve.wait_ge(index_added, h + 1)
                    dve.wait_ge(dve_chain, chain.value())

            def item_late(items, tick):
                if tick < 0 or tick >= len(items) or not items[tick] or items[tick][0] != "sb":
                    return
                s = sm[:, tick % 3, :]
                u = aux[:, tick % 2, :]
                dve.wait_ge(log_ready, count_upto(items, tick, lambda k: k == "sb"))
                chain(dve.scalar_tensor_tensor(u, s, 0.0, u, ALU.max, ALU.add))
                chain.also(dve.tensor_tensor_scan(run[:, 0:P][:, ::-1], u[:, 0:P][:, ::-1], u[:, 0:P][:, ::-1], 0.0,
                                                  ALU.add, ALU.bypass))
                chain(dve.tensor_tensor_scan(run[:, P:3 * P][:, ::-1], u[:, P:3 * P][:, ::-1], u[:, P:3 * P][:, ::-1],
                                             0.0, ALU.add, ALU.bypass))
                dve.tensor_tensor(s, s, run[:, :], ALU.subtract).then_inc(stick_ready, 1)

            def item_y(blk, items, tick):
                if tick < 0 or tick >= len(items) or not items[tick] or items[tick][0] not in HEADS:
                    return
                kind, h = items[tick]
                e = count_upto(items, tick, lambda k: k in HEADS)
                dve.wait_ge(pv_ready, e)
                y = y1 if blk == 1 else y2
                c = {"fox": 0, "sb": 384, "dsa": 768, "swa": 0, "moba": 512}[kind] + h * HD
                src = ps[:, 6 + e % 2, 0:P].rearrange("p (t d) -> p t d", t=NT)
                out = y[:, :, c:c + HD]
                if kind == "sb":
                    dve.tensor_copy(out, src).then_inc(y_done, 1)
                    return
                r = rowsum[:, tick, :]
                if kind == "swa":
                    chain(dve.tensor_tensor(r, r, sinkexp[:, tick, :], ALU.add))
                chain(dve.reciprocal(r, r))
                dve.tensor_tensor(out, src, r.unsqueeze(2).broadcast_to([P, NT, HD]), ALU.mult).then_inc(y_done, 1)

            def ticks(l, blk, items, gates, n0):
                for tick in range(max(len(items) + 4, gates + 1)):
                    item_late(items, tick - 1)
                    item_y(blk, items, tick - 4)
                    if tick < len(items) and items[tick]:
                        item_early(blk, items, tick)
                    if tick < gates and tick % 3 == 0:
                        split_low(l, blk, 1, n0 + tick // 3 + 1)
                    before = tick - 1
                    if 0 <= before < gates and (before % 3 == 1 or (blk == 2 and before == gates - 1)):
                        split_low(l, blk, 0, n0 + before // 3 + 2)
                    if tick in TOKEN_WORK[blk]:
                        TOKEN_WORK[blk][tick]()

            def rotate(x1, x2, cos, sin, tmp):
                chain.also(dve.tensor_tensor(tmp[0], x1, cos, ALU.mult))
                chain.also(dve.tensor_tensor(tmp[1], x2, sin, ALU.mult))
                chain.also(dve.tensor_tensor(tmp[2], x2, cos, ALU.mult))
                chain(dve.tensor_tensor(tmp[3], x1, sin, ALU.mult))
                chain.also(dve.tensor_tensor(x1, tmp[0], tmp[1], ALU.subtract))
                chain(dve.tensor_tensor(x2, tmp[2], tmp[3], ALU.add))

            def rotate1(v, heads):
                h = v.rearrange("p t (h d) -> p t h d", d=HD)
                r = consts[:, C_ROPE:C_ROPE + 32].rearrange("p (t c d) -> p t c d", t=NT, c=2)
                shape = [P, NT, heads, ROPE1]
                cos = r[:, :, 0, :].unsqueeze(2).broadcast_to(shape)
                sin = r[:, :, 1, :].unsqueeze(2).broadcast_to(shape)
                rotate(h[:, :, :, 0:ROPE1], h[:, :, :, ROPE1:2 * ROPE1], cos, sin,
                       [rope_tmp[:, i, :, 0:heads, :] for i in range(4)])

            def tokens1():
                dve.wait_ge(proj_copied, 12)
                for t in range(NT):
                    lat, key = tok1[:, t, 3, 0:P], tok1[:, t, 2, DSA * HD:DSA * HD + HD]
                    chain(dve.tensor_tensor(iscore[:, 0:P], lat, lat, ALU.mult))
                    chain(dve.tensor_reduce(ms[:, t:t + 1], iscore[:, 0:P], AX.X, ALU.add))
                    chain(dve.tensor_tensor(iscore[:, P:P + HD], key, key, ALU.mult))
                    chain(dve.tensor_reduce(ms[:, 2 + t:3 + t], iscore[:, P:P + HD], AX.X, ALU.add))
                chain(dve.tensor_scalar(ms[:, 0:2], ms[:, 0:2], 1.0 / P, None, ALU.mult))
                dve.tensor_scalar(ms[:, 2:4], ms[:, 2:4], 1.0 / HD, None, ALU.mult).then_inc(ms_ready, 1)
                bias = par[:, P1_BF:P1_BF + FOX].unsqueeze(1).broadcast_to([P, NT, FOX])
                chain(dve.tensor_tensor(fsp[:, 0, :, :], tok1[:, :, 1, 324:324 + FOX], bias, ALU.add))
                dve.scalar_tensor_tensor(fsp[:, 1, :, :], fsp[:, 0, :, :], -1.0, fsp[:, 0, :, :], ALU.mult,
                                         ALU.max).then_inc(tok_ask, 1)

            def tokens1_forget():
                newton(4, 1.0)
                chain.also(dve.tensor_scalar(tok1[:, 0, 3, 0:P], tok1[:, 0, 3, 0:P], rstd[:, 0:1], None, ALU.mult))
                dve.tensor_scalar(tok1[:, 1, 3, 0:P], tok1[:, 1, 3, 0:P], rstd[:, 1:2], None,
                                  ALU.mult).then_inc(tokens_ready, 1)
                dve.wait_ge(tok_answer, 1)
                chain(dve.tensor_scalar(fsp[:, 2, :, :], fsp[:, 0, :, :], 0.0, None, ALU.min))
                chain(dve.tensor_tensor(fsp[:, 1, :, :], fsp[:, 1, :, :], fsp[:, 2, :, :], ALU.subtract))
                dve.tensor_copy(fcast[:, :, :, :],
                                fsp[:, 1, :, :].rearrange("p t h -> p h t").unsqueeze(3).broadcast_to(
                                    [P, FOX, NT, P])).then_inc(tokens_ready, 1)

            def tokens1_index():
                for t in range(NT):
                    key = tok1[:, t, 2, DSA * HD:DSA * HD + HD]
                    chain(dve.scalar_tensor_tensor(key, key, rstd[:, 2 + t:3 + t], par[:, P1_GIDX:P1_GIDX + HD],
                                                   ALU.mult, ALU.mult))
                rotate1(tok1[:, :, 2, DSA * HD:DSA * HD + HD], 1)
                for c in (0, HD):
                    chain.also(dve.tensor_copy(dup1[:, :, 0, c:c + HD], tok1[:, :, 2, DSA * HD:DSA * HD + HD]))
                rotate1(tok1[:, :, 3, P:P + IDX * HD], IDX)
                dve.drain().then_inc(tokens_ready, 1)

            def tokens1_queries():
                rotate1(tok1[:, :, 2, 0:DSA * HD], DSA)
                dve.drain().then_inc(tokens_ready, 1)

            def tokens1_latent():
                dve.wait_ge(prep_copied, 2)
                rotate1(kvv[:, :, 0:HD], 1)
                chain.also(dve.tensor_copy(dup1[:, :, 1, 0:HD], kvv[:, :, 0:HD]))
                dve.tensor_copy(dup1[:, :, 1, HD:2 * HD], kvv[:, :, 0:HD]).then_inc(tokens_ready, 1)

            def top_rounds(t, rounds):
                c = slice(0, P) if t == 0 else slice(P, 3 * P)
                for _ in range(rounds):
                    chain(dve.max(top8[:, :], iscore[:, c]))
                    chain(dve.match_replace(iscore[:, c], top8[:, :], iscore[:, c], PICKED))

            def finish_selection():
                chain(dve.tensor_scalar(selmask[:, :], iscore[:, :], PICKED / 2, MASKED, ALU.is_gt, ALU.mult))

            def tokens2_squares(c0, heads, copied):
                dve.wait_ge(proj_copied, copied)
                for t in range(NT):
                    v = tok2[:, t, c0:c0 + heads * HD]
                    chain(dve.tensor_tensor(sq2[:, 0:heads * HD], v, v, ALU.mult))
                    chain(dve.tensor_reduce(ms[:, t * heads:(t + 1) * heads],
                                            sq2[:, 0:heads * HD].rearrange("p (h d) -> p h d", d=HD), AX.X, ALU.add))
                dve.tensor_scalar(ms[:, 0:NT * heads], ms[:, 0:NT * heads], 1.0 / HD, None,
                                  ALU.mult).then_inc(ms_ready, 1)

            def tokens2_scale(c0, heads, groups, t):
                v = tok2[:, t, c0:c0 + heads * HD].rearrange("p (h d) -> p h d", d=HD)
                r = rstd[:, t * heads:(t + 1) * heads].unsqueeze(2).broadcast_to([P, heads, HD])
                chain(dve.tensor_tensor(v, v, r, ALU.mult))
                h0 = 0
                for g, n in groups:
                    gain = par[:, P2_QK + g * HD:P2_QK + (g + 1) * HD].unsqueeze(1).broadcast_to([P, n, HD])
                    chain.also(dve.tensor_tensor(v[:, h0:h0 + n, :], v[:, h0:h0 + n, :], gain, ALU.mult))
                    h0 += n
                dve.wait_ge(dve_chain, chain.value())

            def tokens2_turn(c0, heads, t):
                v = tok2[:, t, c0:c0 + heads * HD].rearrange("p (h d) -> p h d", d=HD)
                shape = [P, heads, ROPE2]
                cos = rope2[:, t, 0, :].unsqueeze(1).broadcast_to(shape)
                sin = rope2[:, t, 1, :].unsqueeze(1).broadcast_to(shape)
                rotate(v[:, :, 0:ROPE2], v[:, :, ROPE2:HD], cos, sin,
                       [rope_tmp2[:, i, 0:heads * ROPE2].rearrange("p (h d) -> p h d", d=ROPE2) for i in range(4)])

            def tokens2_a():
                tokens2_squares(0, 10, 8)

            def tokens2_a_rotate():
                newton(NT * 10, 1.0)
                for t in range(NT):
                    tokens2_scale(0, 10, [(0, SWA), (1, 2)], t)
                    tokens2_turn(0, 10, t)
                for g in range(2):
                    key = tok2[:, :, 512 + g * HD:512 + (g + 1) * HD]
                    chain.also(dve.tensor_copy(dup2[:, :, g, 0:HD], key))
                    chain.also(dve.tensor_copy(dup2[:, :, g, HD:2 * HD], key))
                dve.drain().then_inc(tokens_ready, 1)

            def tokens2_b(t, turn):
                if t == 0 and not turn:
                    newton(NT * 16, 1.0)
                if turn:
                    tokens2_turn(768, 16, t)
                else:
                    tokens2_scale(768, 16, [(2, MOBA), (3, MOBA)], t)
                if turn and t == NT - 1:
                    dve.drain().then_inc(tokens_ready, 1)

            TOKEN_WORK = {
                1: {3: tokens1_latent,
                    10: lambda: top_rounds(0, 3), 11: lambda: top_rounds(0, 3), 12: lambda: top_rounds(0, 2),
                    13: lambda: top_rounds(1, 3), 14: lambda: top_rounds(1, 3),
                    15: lambda: (top_rounds(1, 2), finish_selection())},
                2: {1: lambda: tokens2_b(0, False), 3: lambda: tokens2_b(0, True),
                    5: lambda: tokens2_b(1, False), 7: lambda: tokens2_b(1, True)}}

            def turn_y(tiles):
                for i in range(0, tiles, 2):
                    w = min(2, tiles - i)
                    seen(yhi_ready, "yhi")
                    dve.scalar_tensor_tensor(ylo[:, i:i + w, :].rearrange("p a b -> p (a b)"),
                                             ps[:, (i // 2) % 4, 0:w * SEQ], 0.5,
                                             yhi[:, i:i + w, :].bitcast(F32).rearrange("p a b -> p (a b)"),
                                             ALU.mult, ALU.subtract).then_inc(ylo_ready, 1)

            def merge(l, blk, walk, n0, branches, gt):
                g = g1 if blk == 1 else g2
                splits = [(k, n0 + i + d) for i in range(6) for k, d in ((1, 1), (0, 2))][:-1]

                def split_until(slot):
                    while splits and splits[0][1] <= slot + 1:
                        split_low(l, blk, *splits.pop(0))

                for f in range(KD):
                    last_slot = walk.tiles[(f + 1) * walk.group - 1][0]
                    split_until(last_slot - 1)
                    sem_, val = walk.mark[f]
                    dve.wait_ge({"a": used[0], "b": used[1], "g": group_done}[sem_], val)
                    dve.wait_ge(gates_ready, f + 1)
                    bank = UP_BANKS[f % 4]
                    for br in range(branches):
                        chain.also(dve.scalar_tensor_tensor(
                            mt[:, br, :], g[:, f * branches + br, :], 1.0,
                            ps[:, bank + br // 2, (br % 2) * SEQ:(br % 2 + 1) * SEQ], ALU.add, ALU.mult))
                    dve.wait_ge(dve_chain, chain.value())
                    for br in range(1, branches):
                        chain(dve.tensor_tensor(mt[:, 0, :], mt[:, 0, :], mt[:, br, :], ALU.add))
                    chain(dve.tensor_copy(hhi[:, f, :], mt[:, 0, :]))
                    dve.tensor_tensor(hlo[:, f, :], mt[:, 0, :], hhi[:, f, :].bitcast(F32),
                                      ALU.subtract).then_inc(merged_ready, 1)
                    dve.wait_ge(merged_ready, f + 1)
                    if splits[0][1] <= last_slot + 1:
                        split_low(l, blk, *splits.pop(0))
                while splits:
                    split_low(l, blk, *splits.pop(0))
                if gt:
                    seen(gain_copied, "gain", 2)
                for t in range(NT):
                    for h in range(2):
                        sum_complete(t, h, used[0], parts_before(SL[blk], 0, n0 + 6))
                        c = slice(h * 512, (h + 1) * 512)
                        if gt:
                            gained_residual(t, h)
                        else:
                            dve.tensor_tensor(x[:, t, c], ps[:, 4 + 2 * t + h, :], x[:, t, c],
                                              ALU.add).then_inc(x_ready, 1)

            def modulation_columns(l, blk):
                dve.wait_ge(params_in, params_of(l, blk))
                chain(dve.tensor_tensor(mod[:, :], mod_raw[:, bass.ds(l * MOD, MOD)],
                                        par[:, P2_BADA:P2_BADA + MOD], ALU.add))
                chain(dve.tensor_scalar(small[:, 32:40], par[:, P2_SINK:P2_SINK + SWA], -1.0, None, ALU.mult))
                chain(dve.scalar_tensor_tensor(ncol[:, 0:KD], mod[:, 8:16], 1.0, par[:, P2_G:P2_G + 8],
                                               ALU.add, ALU.mult))
                dve.scalar_tensor_tensor(ncol[:, KD:2 * KD], mod[:, 32:40], 1.0, par[:, P2_G + 8:P2_G + 16],
                                         ALU.add, ALU.mult).then_inc(mod_ready, 1)
                dve.wait_ge(mod_ready, 1)

            own = Count(dve, setup_vector)
            own(dve.memset(small[:, 60:61], EPS))
            own(dve.memset(small[:, 62:64], 1.0))
            own(dve.tensor_copy(ones_r[:, :], small[:, 62:64]))
            dve.wait_ge(small_in, 32)
            own(dve.tensor_copy(small[:, 4:4 + NT], small[:, 0:NT].bitcast(I32)))
            dve.memset(small[:, 61:62], 0.0).then_inc(setup_chain, 1)
            dve.wait_ge(setup_chain, 2)
            own(dve.tensor_scalar(small[:, 16:24], small[:, 16:24], 1.0, None, ALU.add))
            own(dve.reciprocal(small[:, 16:24], small[:, 16:24]))
            own(dve.tensor_tensor(csilu[:, :], csilu[:, :], small[:, 16:24], ALU.mult))
            dve.wait_ge(consts_in, 16)
            k_, tmp = angle_temp[:, 0, :, :, :], angle_temp[:, 1, :, :, :]
            for t in range(NT):
                own(dve.tensor_scalar(rope2[:, t, :, :],
                                      consts[:, C_INVF:C_INVF + ROPE2].unsqueeze(1).broadcast_to([P, 2, ROPE2]),
                                      small[:, 4 + t:5 + t], None, ALU.mult))
            for i, quarter in ((0, 0.25), (1, 0.0)):
                own(dve.tensor_scalar(k_[:, :, i, :], rope2[:, :, i, :], 1.0 / (2 * np.pi), quarter,
                                      ALU.mult, ALU.add))
            own(dve.tensor_scalar(k_, k_, 12582912.0, None, ALU.add))
            own(dve.tensor_scalar(k_, k_, 12582912.0, None, ALU.subtract))
            for part in TWO_PI:
                own(dve.tensor_scalar(tmp, k_, part, None, ALU.mult))
                own(dve.tensor_tensor(rope2[:, :, :, :], rope2[:, :, :, :], tmp, ALU.subtract))
            own(dve.tensor_scalar(rope2[:, :, 0, :], rope2[:, :, 0, :], 0.5 * np.pi, None, ALU.add))
            dve.tensor_scalar(rope2[:, :, :, :], rope2[:, :, :, :], 3.1415925, -3.1415925, ALU.min,
                              ALU.max).then_inc(angles_ready, 1)
            dve.wait_ge(x_in, 16)

            for blk in (1, 2):
                if blk == 2:
                    dve.wait_ge(tables_ready, 1)
                    dve.wait_ge(final_gain_in, 16)
                    dve.wait_ge(between, 4)
                    last_norm = Count(dve, between)
                    last_norm.n = 4
                    w = slice(0, NT)
                    last_norm(dve.tensor_scalar(ms[:, w], ms[:, w], 1.0 / D, EPS, ALU.mult, ALU.add))
                    last_norm(dve.tensor_tensor(rt[:, w], rs0[:, w], rs0[:, w], ALU.mult))
                    last_norm(dve.tensor_tensor(rt[:, w], rt[:, w], ms[:, w], ALU.mult))
                    last_norm(dve.tensor_scalar(rt[:, w], rt[:, w], -0.5, 1.5, ALU.mult, ALU.add))
                    last_norm(dve.tensor_tensor(rstd[:, w], rs0[:, w], rt[:, w], ALU.mult))
                    for t in range(NT):
                        last_norm(dve.scalar_tensor_tensor(x[:, t, :], x[:, t, :], rstd[:, t:t + 1], gfin[:, :],
                                                           ALU.mult, ALU.mult))
                with dve.Fori(0, LAYERS) as l:
                    state.clear()
                    chain.n = 0
                    dve.sem_inc(x_ready, 4)
                    state["x"] = 4
                    starts = dict(between=lambda: split_low(l, blk, 0, 0),
                                  after=lambda: (split_low(l, blk, 1, 0), split_low(l, blk, 0, 1)))
                    if blk == 1:
                        g = lambda k: par[:, P1_G + k:P1_G + k + 1]
                        norm(g, **starts)
                        feed_forward(l, 1, 0, FF1, 2)
                        norm(lambda k: g(8 + k), between=lambda: keep_ada(l, 0), after=lambda: (split_low(l, 1, 1, FF1), split_low(l, 1, 0, FF1 + 1)))
                        projections(l, 1, FF1, 8, {4: tokens1, 5: tokens1_forget, 6: tokens1_index,
                                                   7: tokens1_queries})
                        chain(dve.memset(y1[:, :, 384 + SB * HD:768], 0.0))
                        chain(dve.memset(y1[:, :, 768 + DSA * HD:YT1 * P], 0.0))
                        ticks(l, 1, schedule1(), 24, FF1 + 8)
                        turn_y(YT1)
                        merge(l, 1, Walk(SLOTS1, FF1 + 16, 3, YT1, G_AT[1]), FF1 + 16, 3, False)
                        norm(lambda k: g(16 + k), after=lambda: split_low(l, 1, 0, FF1 + 23))
                        feed_forward(l, 1, FF1 + 22, FF1, 2)
                        keep_ada(l, 1)
                    else:
                        modulation_columns(l, blk)
                        norm(lambda k: ncol[:, k:k + 1], lambda k: mod[:, k:k + 1], **starts)
                        gain_diagonals(16, 0)
                        projections(l, 2, 0, 6, {2: tokens2_a, 3: tokens2_a_rotate, 4: lambda: gain_diagonals(16, 1),
                                                 5: lambda: tokens2_squares(768, 16, 20)})
                        ticks(l, 2, schedule2(), 16, 6)
                        turn_y(YT2)
                        merge(l, 2, Walk(SLOTS2, 12, 3, YT2, G_AT[2]), 12, 2, True)
                        norm(lambda k: ncol[:, KD + k:KD + k + 1], lambda k: mod[:, 24 + k:25 + k],
                             after=lambda: split_low(l, 2, 0, 19))
                        feed_forward(l, 2, 18, FF2, 1, {0: lambda: gain_diagonals(40, 0),
                                                        1: lambda: gain_diagonals(40, 1)})
                    close_layer(dve, l, blk)


def lay_out(inputs):
    a = {}

    def tiles(w, cols):
        n_l, k, n = w.shape
        return w.reshape(n_l, k // P, P, n // cols, cols).transpose(0, 3, 2, 1, 4)

    def pad(w, rows=None, cols=None):
        out = np.zeros((w.shape[0], rows or w.shape[1], cols or w.shape[2]), w.dtype)
        out[:, :w.shape[1], :w.shape[2]] = w
        return out

    def parts(name, stream, count):
        n_l = stream.shape[0]
        full = np.zeros((n_l, count * 24, P, P), stream.dtype)
        full[:, :stream.shape[1]] = stream
        full = full.reshape(n_l, count, 24, P, P).transpose(0, 1, 3, 2, 4)
        a[name + "_a"] = full[:, :, :, :16].reshape(n_l, count, P, 16 * P)
        a[name + "_b"] = full[:, :, :, 16:].reshape(n_l, count, P, 8 * P)

    def as_tiles(w):
        n_l, k, n = w.shape
        return w.reshape(n_l, k // P, P, n // P, P).transpose(0, 3, 1, 2, 4)

    for name, gu, down in (("w1_ffn_a", "w_ffn1_gu", "w_ffn1_down"), ("w1_ffn_b", "w_ffn2_gu", "w_ffn2_down")):
        t = as_tiles(inputs[gu])
        both = np.concatenate([t[:, :FF1], t[:, FF1:]], axis=2)
        a[name + "_a"] = both.transpose(0, 1, 3, 2, 4).reshape(LAYERS, FF1, P, 16 * P)
        a[name + "_b"] = inputs[down].reshape(LAYERS, FF1, P, D)
    t = as_tiles(inputs["w_up_2"])
    a["w2_ffn_a"] = t.transpose(0, 1, 3, 2, 4).reshape(LAYERS, FF2, P, 8 * P)
    a["w2_ffn_b"] = inputs["w_down_2"].reshape(LAYERS, FF2, P, D)

    w, at, cut = inputs["w_in"], 0, {}
    for key, n in (("qa", 384), ("ka", 384), ("va", 384), ("fa", FOX), ("qb", 320), ("kb", 320), ("vb", 320),
                   ("qc", 320), ("ckv", 128), ("qi", 256), ("ki", 64), ("wi", IDX), ("gates", 3 * D)):
        cut[key] = w[:, :, at:at + n]
        at += n
    groups = [("ckv", "qi"), ("qc", "ki"), ("vb", "wi", "fa"), ("va",), ("qa",), ("ka",), ("qb",), ("kb",)]
    slots = np.stack([pad(np.concatenate([cut[k] for k in g], axis=2), cols=384) for g in groups], axis=1)

    def row_parts(name, slots):
        n_l, n = slots.shape[:2]
        s = slots.reshape(n_l, n, KD, P, 384).transpose(0, 1, 3, 2, 4)
        a[name + "_a"] = s[..., :256].reshape(n_l, n, P, KD * 256)
        a[name + "_b"] = s[..., 256:].reshape(n_l, n, P, KD * P)

    row_parts("w1_proj", slots)
    g = as_tiles(cut["gates"]).reshape(LAYERS, 3, KD, KD, P, P).transpose(0, 2, 1, 3, 4, 5)
    parts("w1_gate", g.reshape(LAYERS, 192, P, P), 8)
    up = np.concatenate([pad(inputs["w_up_fox"], rows=384), pad(inputs["w_up_sb"], rows=384),
                         pad(inputs["w_up_dsa"], rows=384)], axis=1)
    parts("w1_up", as_tiles(up).reshape(LAYERS, 72, P, P), 3)

    def out_parts(name, w):
        parts(name, w.reshape(LAYERS, KD, P, KD, P).transpose(0, 1, 3, 2, 4).reshape(LAYERS, 64, P, P), 3)

    out_parts("w1_out", inputs["w_out"])
    out_parts("w2_out", inputs["w_out_2"])
    w = inputs["w_in_2"]
    row_parts("w2_proj", w[:, :, :W_IN2].reshape(LAYERS, D, 6, 384).transpose(0, 2, 1, 3))
    g = as_tiles(w[:, :, W_IN2:]).reshape(LAYERS, 2, KD, KD, P, P).transpose(0, 2, 1, 3, 4, 5)
    parts("w2_gate", g.reshape(LAYERS, 128, P, P), 6)
    up = np.concatenate([inputs["w_o_swa_2"], inputs["w_o_moba_2"]], axis=1)
    parts("w2_up", as_tiles(up).reshape(LAYERS, 64, P, P), 3)
    a["w2_ada"] = tiles(inputs["w_ada_2"], ADA).reshape(LAYERS, 2 * ADA_CHUNKS, P, 2, KD // 2, ADA).transpose(
        0, 1, 3, 2, 4, 5)

    def cols(v):
        return v.reshape(v.shape[0], -1, P).transpose(0, 2, 1)

    def rows(v):
        return np.broadcast_to(v[:, None, :], (v.shape[0], P, v.shape[1]))

    a["params1"] = np.concatenate([cols(inputs["g_ffn1"]), cols(inputs["g_mix"]), cols(inputs["g_ffn2"]),
                                   cols(inputs["g_kv_latent"]), rows(inputs["b_forget"]), rows(inputs["g_idx_k"]),
                                   inputs["w_kv_up"]], axis=2)
    a["params2"] = np.concatenate([cols(inputs["rms_mix_2"]), cols(inputs["rms_mlp_2"]), cols(inputs["b_ada_2"]),
                                   rows(inputs["q_norm_swa_2"]), rows(inputs["k_norm_swa_2"]),
                                   rows(inputs["q_norm_moba_2"]), rows(inputs["k_norm_moba_2"]),
                                   rows(inputs["swa_sinks_2"])], axis=2)
    a["x"] = inputs["x"].reshape(SEQ, D)
    a["g_final"] = np.broadcast_to(inputs["g_final"], (P, D))
    a["c"] = inputs["c_2"].reshape(KD, P).T
    a["positions"] = inputs["positions_2"].reshape(NT, P).T
    return a


def shape_constants():
    f = np.float32
    q, k = np.arange(P)[:, None], np.arange(P)[None, :]
    zero, full = np.zeros((P, P), f), np.full((P, P), MASKED, f)
    causal = np.where(k <= q, 0, MASKED).astype(f)
    strict = np.where(k < q, 0, MASKED).astype(f)
    beyond = np.where(k > q, 0, MASKED).astype(f)
    assert WINDOW == P
    chunk = np.where(k // CHUNK <= q // CHUNK, 0, MASKED).astype(f)
    upper = (q <= k).astype(f)
    inv = (f(500000.0) ** (-np.arange(0, 16, 2, dtype=f) / f(16))).astype(f)
    ang = np.arange(SEQ, dtype=f)[:, None] * inv[None, :]
    rope = np.stack([np.cos(ang), np.sin(ang)], axis=1).reshape(NT, P, 2 * ROPE1).transpose(1, 0, 2).reshape(P, 32)
    inv2 = (f(10000.0) ** (-np.arange(ROPE2, dtype=f) / f(ROPE2))).astype(f)
    out = np.concatenate([np.eye(P, dtype=f), causal, zero, causal, strict, zero, strict, chunk, zero, chunk,
                          causal, beyond, causal, upper, np.ones((P, P), f), rope.astype(f),
                          np.broadcast_to(inv2, (P, ROPE2))], axis=1)
    assert out.shape == (P, C_END)
    return np.ascontiguousarray(out, dtype=f)


def kernel(**inputs):
    import numpy as _np
    import concourse.bacc as _bacc
    from concourse import mybir as _mybir
    from concourse.bass_utils import run_bass_kernel_spmd as _run

    nc = _bacc.Bacc("TRN2", target_bir_lowering=False, num_devices=1)
    laid = lay_out({k: _np.asarray(v) for k, v in inputs.items()})
    laid["consts"] = shape_constants()
    arrays, aps = {}, {}
    for name, v in laid.items():
        v = _np.ascontiguousarray(v)
        arrays[f"in_{name}"] = v
        aps[name] = nc.dram_tensor(f"in_{name}", v.shape, _mybir.dt.from_np(v.dtype), kind="ExternalInput").ap()
    aps["out"] = nc.dram_tensor("out_0", (SEQ, D), _mybir.dt.float32, kind="ExternalOutput").ap()
    build(nc, aps)
    r = _run(nc, [arrays], core_ids=[0])
    return r.results[0]["out_0"].reshape(1, SEQ, D)
```
